# Optimizing a Trainium2 kernel written in Bass

```python
import math
import jax, jax.numpy as jnp
from jax import lax
import numpy as np

D_MODEL = 1024
BATCH = 1
SEQ = 512
DEPTH = 1

D_MIX = D_MODEL
HEAD_DIM = 64
N_Q_HEADS = 8
N_KV_HEADS = 2
Q_PER_KV = N_Q_HEADS // N_KV_HEADS
D_ATTN = N_Q_HEADS * HEAD_DIM
D_CONV = D_MIX - D_ATTN
CONV_WIDTH = 31
WINDOW = 128
BLOCK = 128
N_BUCKETS = 32
MAX_EXACT = N_BUCKETS // 2
MAX_DISTANCE = 128
D_FF = int(math.ceil(8 * D_MODEL / 3 / 256) * 256)
EPS = 1e-6
D_Q = N_Q_HEADS * HEAD_DIM
D_KV = N_KV_HEADS * HEAD_DIM
D_IN = D_Q + 2 * D_KV + 2 * D_CONV


def rms_norm(x, g):
    xf = x.astype(jnp.float32)
    y = xf * lax.rsqrt(jnp.mean(xf * xf, axis=-1, keepdims=True) + EPS)
    return (y * g.astype(jnp.float32)).astype(x.dtype)

def layer_norm(x, g, b):
    xf = x.astype(jnp.float32)
    mu = jnp.mean(xf, axis=-1, keepdims=True)
    var = jnp.mean(jnp.square(xf - mu), axis=-1, keepdims=True)
    y = (xf - mu) * lax.rsqrt(var + EPS)
    return (y * g.astype(jnp.float32) + b.astype(jnp.float32)).astype(x.dtype)

def t5_causal_bucket(dist):
    is_small = dist < MAX_EXACT
    d = jnp.maximum(dist, 1).astype(jnp.float32)
    large = MAX_EXACT + (jnp.log(d / MAX_EXACT) / math.log(MAX_DISTANCE / MAX_EXACT)
                         * (N_BUCKETS - MAX_EXACT)).astype(jnp.int32)
    large = jnp.minimum(large, N_BUCKETS - 1)
    return jnp.where(is_small, dist, large)

def conformer_conv(u, conv_dw, conv_dw_b, conv_ln_g, conv_ln_b, w_conv_pw):
    a, gate = jnp.split(u, 2, axis=-1)
    h = a * jax.nn.sigmoid(gate)
    h = lax.conv_general_dilated(
        h, conv_dw[:, None, :].astype(h.dtype), window_strides=(1,),
        padding=[(CONV_WIDTH - 1, 0)],
        dimension_numbers=("NWC", "WIO", "NWC"),
        feature_group_count=D_CONV) + conv_dw_b
    h = jax.nn.silu(layer_norm(h, conv_ln_g, conv_ln_b))
    return h @ w_conv_pw

def sliding_window_attention(q, k, v, attn_sinks, rel_bias):
    B, S = q.shape[0], q.shape[1]
    nb = S // BLOCK
    qb = q.reshape(B, nb, BLOCK, N_KV_HEADS, Q_PER_KV, HEAD_DIM)
    pad = ((0, 0), (BLOCK, 0), (0, 0), (0, 0))
    kp, vp = jnp.pad(k, pad), jnp.pad(v, pad)

    def band(t):
        prev = t[:, :S].reshape(B, nb, BLOCK, N_KV_HEADS, HEAD_DIM)
        cur = t[:, BLOCK:].reshape(B, nb, BLOCK, N_KV_HEADS, HEAD_DIM)
        return jnp.concatenate([prev, cur], axis=2)

    kb, vb = band(kp), band(vp)
    scale = 1.0 / math.sqrt(HEAD_DIM)
    s = jnp.einsum("bnqhgd,bnkhd->bnhgqk", qb, kb).astype(jnp.float32) * scale

    qi = jnp.arange(BLOCK)[:, None]
    kj = jnp.arange(2 * BLOCK)[None, :]
    dist = qi + BLOCK - kj
    in_band = (dist >= 0) & (dist < WINDOW)
    bucket = t5_causal_bucket(jnp.maximum(dist, 0))
    bias = rel_bias.astype(jnp.float32)[bucket]
    bias = jnp.transpose(bias, (2, 0, 1)).reshape(N_KV_HEADS, Q_PER_KV, BLOCK, 2 * BLOCK)
    blk = jnp.arange(nb)[:, None, None]
    valid = in_band[None] & ((blk > 0) | (kj[None] >= BLOCK))
    s = jnp.where(valid[None, :, None, None], s + bias, -jnp.inf)

    sink = attn_sinks.astype(jnp.float32).reshape(N_KV_HEADS, Q_PER_KV, 1, 1)
    m = jnp.maximum(jnp.max(s, axis=-1, keepdims=True), sink)
    p = jnp.exp(s - m)
    denom = jnp.sum(p, axis=-1, keepdims=True) + jnp.exp(sink - m)
    p = (p / denom).astype(v.dtype)
    o = jnp.einsum("bnhgqk,bnkhd->bnqhgd", p, vb)
    return o.reshape(B, S, N_Q_HEADS * HEAD_DIM)

def first_inputs(seed: int = 0) -> dict:
    key = jax.random.key(seed)
    ks = jax.random.split(key, 20)
    f = jnp.float32
    nrm = lambda k, shp, sc: jax.random.normal(k, shp, f) * sc
    gain = lambda k, n: 1.0 + 0.05 * jax.random.normal(k, (n,), f)
    return {
        "x": jax.random.normal(ks[0], (BATCH, SEQ, D_MODEL), f),
        "mix_pre_g": gain(ks[1], D_MODEL),
        "mix_post_g": gain(ks[2], D_MODEL),
        "ffn_pre_g": gain(ks[3], D_MODEL),
        "ffn_post_g": gain(ks[4], D_MODEL),
        "w_in": nrm(ks[5], (D_MODEL, D_IN), D_MODEL ** -0.5),
        "conv_dw": nrm(ks[6], (CONV_WIDTH, D_CONV), CONV_WIDTH ** -0.5),
        "conv_dw_b": nrm(ks[7], (D_CONV,), 0.02),
        "conv_ln_g": gain(ks[8], D_CONV),
        "conv_ln_b": nrm(ks[9], (D_CONV,), 0.02),
        "w_conv_pw": nrm(ks[10], (D_CONV, D_CONV), D_CONV ** -0.5),
        "attn_sinks": nrm(ks[11], (N_Q_HEADS,), 0.5),
        "rel_bias": nrm(ks[12], (N_BUCKETS, N_Q_HEADS), 0.5),
        "w_out": nrm(ks[13], (D_MIX, D_MODEL), D_MIX ** -0.5),
        "w_gate": nrm(ks[14], (D_MODEL, D_FF), D_MODEL ** -0.5),
        "w_up": nrm(ks[15], (D_MODEL, D_FF), D_MODEL ** -0.5),
        "w_down": nrm(ks[16], (D_FF, D_MODEL), D_FF ** -0.5),
    }

def first_block(x, mix_pre_g, mix_post_g, ffn_pre_g, ffn_post_g, w_in, conv_dw, conv_dw_b,
              conv_ln_g, conv_ln_b, w_conv_pw, attn_sinks, rel_bias, w_out,
              w_gate, w_up, w_down):
    B, S, _ = x.shape
    h = x
    for _layer in range(DEPTH):
        hn = rms_norm(h, mix_pre_g)
        proj = hn @ w_in
        q = proj[..., :D_Q].reshape(B, S, N_Q_HEADS, HEAD_DIM)
        k = proj[..., D_Q:D_Q + D_KV].reshape(B, S, N_KV_HEADS, HEAD_DIM)
        v = proj[..., D_Q + D_KV:D_Q + 2 * D_KV].reshape(B, S, N_KV_HEADS, HEAD_DIM)
        u = proj[..., D_Q + 2 * D_KV:]
        attn_out = sliding_window_attention(q, k, v, attn_sinks, rel_bias)
        conv_out = conformer_conv(u, conv_dw, conv_dw_b, conv_ln_g, conv_ln_b, w_conv_pw)
        mixed = jnp.concatenate([attn_out, conv_out], axis=-1) @ w_out
        h = h + rms_norm(mixed, mix_post_g)
        hn = rms_norm(h, ffn_pre_g)
        ff = (jax.nn.silu(hn @ w_gate) * (hn @ w_up)) @ w_down
        h = h + rms_norm(ff, ffn_post_g)
    return h


A_GROUPS = 4
A_GROUP_DIM = 128
A_WIDTH = A_GROUPS * A_GROUP_DIM
CHUNK = 128
N_HEADS = 4
HEAD_DIM_2 = 128
B_WIDTH = N_HEADS * HEAD_DIM_2
KV_LATENT = 256
ROT_DIM = HEAD_DIM_2 // 4
IDX_HEADS = 4
IDX_DIM = 64
IDX_ROT = IDX_DIM // 4
TOPK_MAX = 256
Q_BLOCK = 128
ROPE_THETA = 500000.0
N_BRANCHES = 2
PEER_HEADS = 8
PEER_KEY_DIM = 256
PEER_HALF = PEER_KEY_DIM // 2
N_KEYS = 128
N_EXPERTS = N_KEYS * N_KEYS
PEER_TOPK = 16
PEER_BLOCK = 128

SPLITS = (A_WIDTH, A_WIDTH, B_WIDTH, KV_LATENT, IDX_HEADS * IDX_DIM, IDX_DIM, IDX_HEADS, N_BRANCHES * D_MODEL)
IN_WIDTH = sum(SPLITS)
SPLIT_OFFSETS = tuple(int(o) for o in np.cumsum(SPLITS)[:-1])


def rms_norm_2(x, g):
    xf = x.astype(jnp.float32)
    y = xf * lax.rsqrt(jnp.mean(xf * xf, axis=-1, keepdims=True) + EPS)
    return (y * g.astype(jnp.float32)).astype(x.dtype)

def layer_norm_2(x, g, b):
    xf = x.astype(jnp.float32)
    mu = jnp.mean(xf, axis=-1, keepdims=True)
    xc = xf - mu
    y = xc * lax.rsqrt(jnp.mean(xc * xc, axis=-1, keepdims=True) + EPS)
    return (y * g.astype(jnp.float32) + b.astype(jnp.float32)).astype(x.dtype)

def partial_rope(x, pos, rot_dim):
    half = rot_dim // 2
    inv = jnp.power(jnp.float32(ROPE_THETA), -jnp.arange(half, dtype=jnp.float32) * 2.0 / rot_dim)
    ang = pos.astype(jnp.float32)[..., None] * inv
    cos = jnp.cos(ang)[:, :, None, :]
    sin = jnp.sin(ang)[:, :, None, :]
    xr = x[..., :rot_dim].astype(jnp.float32)
    x1, x2 = xr[..., :half], xr[..., half:]
    rot = jnp.concatenate([x1 * cos - x2 * sin, x2 * cos + x1 * sin], axis=-1)
    return jnp.concatenate([rot.astype(x.dtype), x[..., rot_dim:]], axis=-1)

def chunked_spatial_gating(u, v, v_g, v_b, w_s, b_s):
    bsz, s, _ = u.shape
    u = jax.nn.gelu(u)
    v = layer_norm_2(jax.nn.gelu(v), v_g, v_b)
    v = v.reshape(bsz, s // CHUNK, CHUNK, A_GROUPS, A_GROUP_DIM)
    causal = jnp.tril(jnp.ones((CHUNK, CHUNK), dtype=bool))
    w = jnp.where(causal[None], w_s, jnp.zeros_like(w_s))
    z = jnp.einsum('gts,bcsgd->bctgd', w, v) + b_s.T[None, None, :, :, None]
    return u * z.reshape(bsz, s, A_WIDTH)

def dsa_attention(q, k, v, q_idx, k_idx, w_idx):
    bsz, s = q.shape[:2]
    n_sel = min(TOPK_MAX, s // 4)
    nblk = s // Q_BLOCK
    key_pos = jnp.arange(s)

    def to_blocks(a):
        return a.reshape(bsz, nblk, Q_BLOCK, *a.shape[2:]).swapaxes(0, 1)

    def gather_rows(table, idx):
        return table[idx]

    def block_fn(args):
        blk, qb, qib, wib = args
        q_pos = blk * Q_BLOCK + jnp.arange(Q_BLOCK)
        causal = key_pos[None, :] <= q_pos[:, None]
        logits = jnp.einsum('bqhd,bsd->bqhs', qib, k_idx, preferred_element_type=jnp.float32) * (IDX_DIM ** -0.5)
        scores = jnp.einsum('bqh,bqhs->bqs', wib.astype(jnp.float32), jax.nn.relu(logits))
        scores = jnp.where(causal[None], scores, -jnp.inf)
        _, idx = lax.top_k(scores, n_sel)
        valid = idx <= q_pos[None, :, None]
        k_sel = jax.vmap(gather_rows)(k, idx)
        v_sel = jax.vmap(gather_rows)(v, idx)
        att = jnp.einsum('bqhd,bqnd->bqhn', qb, k_sel, preferred_element_type=jnp.float32) * (HEAD_DIM_2 ** -0.5)
        att = jnp.where(valid[:, :, None, :], att, jnp.float32(-1e30))
        p = jax.nn.softmax(att, axis=-1).astype(v.dtype)
        return jnp.einsum('bqhn,bqnd->bqhd', p, v_sel)

    out = lax.map(block_fn, (jnp.arange(nblk), to_blocks(q), to_blocks(q_idx), to_blocks(w_idx)))
    return out.swapaxes(0, 1).reshape(bsz, s, B_WIDTH)

def peer(xn, wq, subkeys, u_tab, v_tab):
    bsz, s, d = xn.shape
    q = (xn @ wq).reshape(bsz, s, PEER_HEADS, 2, PEER_HALF)
    sub = jnp.einsum('bshpd,hpnd->bshpn', q, subkeys, preferred_element_type=jnp.float32)
    s_top, i_top = lax.top_k(sub, PEER_TOPK)
    cand = (s_top[..., 0, :, None] + s_top[..., 1, None, :]).reshape(bsz, s, PEER_HEADS, PEER_TOPK * PEER_TOPK)
    cand_idx = (i_top[..., 0, :, None] * N_KEYS + i_top[..., 1, None, :]).reshape(bsz, s, PEER_HEADS, PEER_TOPK * PEER_TOPK)
    best, pos = lax.top_k(cand, PEER_TOPK)
    expert = jnp.take_along_axis(cand_idx, pos, axis=-1)
    gate = jax.nn.softmax(best, axis=-1)
    nb = (bsz * s) // PEER_BLOCK
    hk = PEER_HEADS * PEER_TOPK
    xt = xn.reshape(nb, PEER_BLOCK, d)
    et = expert.reshape(nb, PEER_BLOCK, hk)
    gt = gate.reshape(nb, PEER_BLOCK, hk)

    def blk(args):
        xb, eb, gb = args
        ub = u_tab[eb]
        vb = v_tab[eb]
        a = jax.nn.gelu(jnp.einsum('td,ted->te', xb, ub, preferred_element_type=jnp.float32))
        return jnp.einsum('te,ted->td', (gb * a).astype(vb.dtype), vb)

    y = lax.map(blk, (xt, et, gt))
    return y.reshape(bsz, s, d)

def second_inputs(seed: int = 0) -> dict:
    key = jax.random.key(seed)
    ks = jax.random.split(key, 24)
    f32 = jnp.float32
    L = DEPTH
    nrm = lambda k, shape, scale: jax.random.normal(k, shape, f32) * scale
    x = jax.random.normal(ks[0], (BATCH, SEQ, D_MODEL), f32)
    positions = jnp.broadcast_to(jnp.arange(SEQ, dtype=jnp.int32)[None, :], (BATCH, SEQ))
    return {
        "x": x,
        "positions": positions,
        "norm1_g": 1.0 + nrm(ks[1], (L, D_MODEL), 0.02),
        "w_in": nrm(ks[2], (L, D_MODEL, IN_WIDTH), D_MODEL ** -0.5),
        "v_norm_g": 1.0 + nrm(ks[3], (L, A_WIDTH), 0.02),
        "v_norm_b": nrm(ks[4], (L, A_WIDTH), 0.02),
        "spatial_w": nrm(ks[5], (L, A_GROUPS, CHUNK, CHUNK), CHUNK ** -0.5),
        "spatial_b": 1.0 + nrm(ks[6], (L, A_GROUPS, CHUNK), 0.1),
        "kv_norm_g": 1.0 + nrm(ks[7], (L, KV_LATENT), 0.02),
        "w_uk": nrm(ks[8], (L, KV_LATENT, HEAD_DIM_2), KV_LATENT ** -0.5),
        "w_uv": nrm(ks[9], (L, KV_LATENT, HEAD_DIM_2), KV_LATENT ** -0.5),
        "q_norm_g": 1.0 + nrm(ks[10], (L, HEAD_DIM_2), 0.02),
        "k_norm_g": 1.0 + nrm(ks[11], (L, HEAD_DIM_2), 0.02),
        "w_a_out": nrm(ks[12], (L, A_WIDTH, D_MODEL), A_WIDTH ** -0.5),
        "w_b_out": nrm(ks[13], (L, B_WIDTH, D_MODEL), B_WIDTH ** -0.5),
        "w_o": nrm(ks[14], (L, D_MODEL, D_MODEL), D_MODEL ** -0.5),
        "norm2_g": 1.0 + nrm(ks[15], (L, D_MODEL), 0.02),
        "peer_wq": nrm(ks[16], (L, D_MODEL, PEER_HEADS * PEER_KEY_DIM), D_MODEL ** -0.5),
        "peer_subkeys": nrm(ks[17], (L, PEER_HEADS, 2, N_KEYS, PEER_HALF), PEER_HALF ** -0.5),
        "peer_u": nrm(ks[18], (L, N_EXPERTS, D_MODEL), D_MODEL ** -0.5),
        "peer_v": nrm(ks[19], (L, N_EXPERTS, D_MODEL), 0.5 * PEER_HEADS ** -0.5),
    }

def second_block(x, positions, norm1_g, w_in, v_norm_g, v_norm_b, spatial_w, spatial_b, kv_norm_g, w_uk, w_uv,
              q_norm_g, k_norm_g, w_a_out, w_b_out, w_o, norm2_g, peer_wq, peer_subkeys, peer_u, peer_v):
    bsz, s, d = x.shape
    h = x
    for l in range(DEPTH):
        xn = rms_norm_2(h, norm1_g[l])
        proj = xn @ w_in[l]
        u, v, q, c_kv, q_idx, k_idx, w_idx, gates = jnp.split(proj, SPLIT_OFFSETS, axis=-1)

        y_a = chunked_spatial_gating(u, v, v_norm_g[l], v_norm_b[l], spatial_w[l], spatial_b[l])

        c_n = rms_norm_2(c_kv, kv_norm_g[l])
        k = rms_norm_2(c_n @ w_uk[l], k_norm_g[l])
        vv = c_n @ w_uv[l]
        qh = rms_norm_2(q.reshape(bsz, s, N_HEADS, HEAD_DIM_2), q_norm_g[l])
        qh = partial_rope(qh, positions, ROT_DIM)
        k = partial_rope(k[:, :, None, :], positions, ROT_DIM)[:, :, 0, :]
        qi = partial_rope(q_idx.reshape(bsz, s, IDX_HEADS, IDX_DIM), positions, IDX_ROT)
        ki = partial_rope(k_idx[:, :, None, :], positions, IDX_ROT)[:, :, 0, :]
        wi = w_idx * (IDX_HEADS ** -0.5)
        y_b = dsa_attention(qh, k, vv, qi, ki, wi)

        g = jax.nn.sigmoid(gates.reshape(bsz, s, N_BRANCHES, d))
        merged = g[:, :, 0, :] * (y_a @ w_a_out[l]) + g[:, :, 1, :] * (y_b @ w_b_out[l])
        h = h + merged @ w_o[l]

        hn = rms_norm_2(h, norm2_g[l])
        h = h + peer(hn, peer_wq[l], peer_subkeys[l], peer_u[l], peer_v[l])
    return h


def setup_inputs(seed=0):
    out = dict(first_inputs(seed))
    for name, value in second_inputs(seed + 1).items():
        if name != "x":
            out[name + "_2"] = value
    return out


def reference(
    x, mix_pre_g, mix_post_g, ffn_pre_g, ffn_post_g, w_in, conv_dw, conv_dw_b, conv_ln_g,
    conv_ln_b, w_conv_pw, attn_sinks, rel_bias, w_out, w_gate, w_up, w_down, positions_2,
    norm1_g_2, w_in_2, v_norm_g_2, v_norm_b_2, spatial_w_2, spatial_b_2, kv_norm_g_2, w_uk_2,
    w_uv_2, q_norm_g_2, k_norm_g_2, w_a_out_2, w_b_out_2, w_o_2, norm2_g_2, peer_wq_2,
    peer_subkeys_2, peer_u_2, peer_v_2,
):
    x = first_block(
        x, mix_pre_g, mix_post_g, ffn_pre_g, ffn_post_g, w_in, conv_dw, conv_dw_b, conv_ln_g,
        conv_ln_b, w_conv_pw, attn_sinks, rel_bias, w_out, w_gate, w_up, w_down,
    )
    return second_block(
        x, positions_2, norm1_g_2, w_in_2, v_norm_g_2, v_norm_b_2, spatial_w_2, spatial_b_2,
        kv_norm_g_2, w_uk_2, w_uv_2, q_norm_g_2, k_norm_g_2, w_a_out_2, w_b_out_2, w_o_2,
        norm2_g_2, peer_wq_2, peer_subkeys_2, peer_u_2, peer_v_2,
    )


_drawn_inputs = setup_inputs


def setup_inputs(seed=0):
    import zlib

    import numpy as np

    out = dict(_drawn_inputs(seed))
    spreads = {}
    factors = {'conv_ln_b': 3.159,
     'attn_sinks': 7.174,
     'norm1_g_2': 5.615,
     'v_norm_g_2': 25.198,
     'v_norm_b_2': 24.584,
     'spatial_b_2': 2.785,
     'kv_norm_g_2': 8.0,
     'q_norm_g_2': 8.0,
     'k_norm_g_2': 8.0,
     'norm2_g_2': 56.396}
    for name, (base, spread) in spreads.items():
        noise = np.random.default_rng([zlib.crc32(name.encode()), seed]).standard_normal(out[name].shape)
        drawn = base * np.exp(spread * noise) if base else spread * noise
        out[name] = __import__('jax').numpy.asarray(drawn.astype(out[name].dtype))
    for name, factor in factors.items():
        out[name] = (out[name] * factor).astype(out[name].dtype)
    return out
```

```python
import math
from contextlib import ExitStack

import numpy as np

import concourse.bass as bass
from concourse import mybir

F32 = mybir.dt.float32
F32R = mybir.dt.float32r
I32 = mybir.dt.int32
U32 = mybir.dt.uint32
ALU = mybir.AluOpType
ACT = mybir.ActivationFunctionType
AX_X = mybir.AxisListType.X

P = 128
T = 512
NT = T // P
D = 1024
KD = D // P
EPS = 1e-6
NEG = -1e30
TAKEN = -3e38
HD = 64
NH = 8
WIN = 128
BUCKETS = 32
TAPS = 31
CC = 4
FF = 2816
KF = FF // P
SKEW = 3 * P
GR = 4
TOPK = min(256, T // 4)
ROUND = float(1.5 * 2 ** 23)
TURN = [6.28125, 0.0019354820251464844, -1.7484556025237907e-07]
PI_BELOW = 3.1415925
NROT = 16 + 8
NEXP = 128
PH = 8
SEL = 16
HS = PH * SEL
EG = 4
NGRP = NEXP // EG
TOK4 = 4

NR, NW = 3, 3
RING = 2
STOP = 3


def t5_bucket(dist):
    exact = BUCKETS // 2
    if dist < exact:
        return dist
    large = np.float32(np.log(np.float32(dist) / np.float32(exact))) / np.float32(math.log(WIN / exact))
    return min(exact + int(np.float32(large) * np.float32(BUCKETS - exact)), BUCKETS - 1)


def shape_constants():
    onehot = np.zeros((BUCKETS + 1, SKEW), np.float32)
    for m in range(SKEW):
        dist = 2 * P - 1 - m
        onehot[t5_bucket(dist) if 0 <= dist < WIN else BUCKETS, m] = 1.0
    inv = [np.power(np.float32(500000.0), -np.arange(n, dtype=np.float32) * np.float32(2.0) / np.float32(2 * n))
           for n in (16, 8)]
    return onehot, np.concatenate(inv).astype(np.float32).reshape(1, NROT)


def block_pair_kernel(nc, A, onehot_rows, inv_freq, out):
    w_in = A["w_in"]
    conv_in = NH * HD + 2 * 2 * HD

    ctx = ExitStack()
    with ctx:
        def sb(name, shape, dt=F32, scope=ctx):
            return scope.enter_context(nc.sbuf_tensor(name, shape, dt))

        sems = {}

        def s(name):
            if name not in sems:
                sems[name] = ctx.enter_context(nc.semaphore(name))
            return sems[name]

        banks = [ctx.enter_context(nc.psum_tensor(f"bank{b}", [P, 512], F32)) for b in range(8)]
        number = {}

        def bank_of(key):
            return banks[number[key] % 8]

        def wait_full(eng, key):
            n = number[key]
            eng.wait_ge(s(f"full{n % 8}"), n // 8 + 1)
            return banks[n % 8]

        def wait_read(eng, key):
            n = number[key]
            eng.wait_ge(s(f"free{n % 8}"), n // 8 + 1)

        def frees(key):
            return s(f"free{number[key] % 8}")

        units = []
        unit_at = {}

        def unit(key, k, n, parts):
            unit_at[key] = len(units)
            units.append((k, n, parts))

        def chunked(w):
            return w.rearrange("(k p) n -> p k n", p=P)

        win = chunked(w_in)
        QW = NH * HD
        for c in range(CC):
            for name, first in (("cg", conv_in + 512), ("ca", conv_in)):
                unit((name, c), KD, P, [(0, win[:, :, first + c * P:first + (c + 1) * P])])
        for kv in range(2):
            cols = win[:, :, QW + kv * HD:QW + (kv + 1) * HD]
            unit(("kk", kv), KD, P, [(0, cols), (HD, cols)])
        unit(("v", 0), KD, P, [(0, win[:, :, QW + 2 * HD:QW + 4 * HD])])
        for c in range(4):
            unit(("q", c), KD, P, [(0, win[:, :, c * P:(c + 1) * P])])
        pw = chunked(A["w_conv_pw"])
        for c in range(2):
            unit(("pw", c), CC, 2 * P, [(0, pw[:, :, c * 2 * P:(c + 1) * 2 * P])])
        wo = chunked(A["w_out"])
        for c in range(KD):
            unit(("wo", c), KD, P, [(0, wo[:, :, c * P:(c + 1) * P])])
        wg, wu, wd = chunked(A["w_gate"]), chunked(A["w_up"]), chunked(A["w_down"])
        for c in range(KF):
            unit(("wg", c), KD, P, [(0, wg[:, :, c * P:(c + 1) * P])])
            unit(("wu", c), KD, P, [(0, wu[:, :, c * P:(c + 1) * P])])
        DOWN = [(0, 8), (8, 16), (16, KF)]
        for c in range(KD):
            for j, (k0, k1) in enumerate(DOWN):
                unit(("wd", c, j), k1 - k0, P, [(0, wd[:, k0:k1, c * P:(c + 1) * P])])
        w2 = chunked(A["w_in_2"][0])
        for c in range(4):
            unit(("u2", c), KD, P, [(0, w2[:, :, c * P:(c + 1) * P])])
        NAT = [("vn", 512), ("qn", 1024), ("ci", 1536)]
        for name, first in (NAT[2], NAT[1], NAT[0]):
            for j in range(4):
                unit((name, j), 2, 512, [(0, w2[:, 2 * j:2 * j + 2, first:first + 512])])
            if name == "ci":
                unit(("kw", 0), KD, 68, [(0, w2[:, :, 2048:2116])])
        for c in range(16):
            unit(("gt", c), KD, P, [(0, w2[:, :, 2116 + c * P:2116 + (c + 1) * P])])
        wa, wb, wo2 = chunked(A["w_a_out_2"][0]), chunked(A["w_b_out_2"][0]), chunked(A["w_o_2"][0])
        for c in range(4):
            unit(("wa", c), 4, 2 * P, [(0, wa[:, :, c * 2 * P:(c + 1) * 2 * P])])
            unit(("wb", c), 4, 2 * P, [(0, wb[:, :, c * 2 * P:(c + 1) * 2 * P])])
        for c in range(KD):
            unit(("wo2", c), KD, P, [(0, wo2[:, :, c * P:(c + 1) * P])])
        wq = chunked(A["peer_wq_2"][0])
        for c in range(2 * PH):
            unit(("wq", c), KD, P, [(0, wq[:, :, c * P:(c + 1) * P])])

        def heads_of(i, per):
            first = (i // 2) * 2 * per + i % 2
            return slice(first, first + 2 * per - 1, 2)

        squares_before = [0, KD, KD + CC, 2 * KD + CC, 3 * KD + CC, 4 * KD + CC, 5 * KD + CC]
        squares_signalled = [n - m for m, n in enumerate(squares_before)]

        if STOP == 1:
            del units[unit_at[("u2", 0)]:]
        if STOP == 2:
            del units[unit_at[("wq", 0)]:]

        ident = sb("ident", [P, P])
        ones = sb("ones", [P, P])
        eps = sb("eps", [P, 1])
        vrows = sb("vrows", [P, P])
        dwrows = sb("dwrows", [P, P])
        vec = sb("vec", [P, 64])
        taps = sb("taps", [P, P])
        hT = sb("hT", [P, KD, T])
        XH = sb("XH", [P, KD, T], F32R)
        XL = sb("XL", [P, KD, T], F32R)
        sq = sb("sq", [P, RING, T])
        rt = sb("rt", [P, T])
        rstd = sb("rstd", [P, T])
        xn = sb("xn", [P, RING, T])
        stream_scope = ctx.enter_context(ExitStack())
        wraw = sb("wraw", [P, NR, 1024], F32, stream_scope)
        WH = sb("WH", [P, NW, 1024], F32R, stream_scope)
        WL = sb("WL", [P, NW, 1024], F32R, stream_scope)
        y = sb("y", [P, KD, T], F32, stream_scope)

        VROWS = [("mix_pre", A["mix_pre_g"], KD), ("mix_post", A["mix_post_g"], KD), ("ffn_pre", A["ffn_pre_g"], KD),
                 ("ffn_post", A["ffn_post_g"], KD), ("norm1", A["norm1_g_2"][0], KD), ("norm2", A["norm2_g_2"][0], KD),
                 ("dw_b", A["conv_dw_b"], CC), ("ln_g", A["conv_ln_g"], CC), ("ln_b", A["conv_ln_b"], CC)]
        vec_col, at = {}, 0
        for name, src, n in VROWS:
            vec_col[name] = at
            at += n
        NV = at

        def vcol(name, c):
            return vec[:, vec_col[name] + c:vec_col[name] + c + 1]

        x_nat = y[:, :, :].rearrange("p (t a) b -> p t (a b)", t=NT)
        with ExitStack() as sc:
            hpad = sb("hpad", [P, CC, TAPS - 1 + T], F32, sc)
            cacc = sb("cacc", [P, CC, T], F32, sc)
            sg = sb("sg", [P, 2, T], F32, sc)
            kk = sb("kk", [P, 2, T], F32, sc)
            v1 = sb("v1", [P, NT, P], F32, sc)
            q1 = sb("q1", [P, 4, T], F32, sc)
            biasT = sb("biasT", [P, NH, 2 * P], F32, sc)
            sc1 = sb("sc1", [P, 2, NH, 2 * P], F32, sc)
            pT1 = sb("pT1", [P, NH, 2, P], F32, sc)
            sinkb = sb("sinkb", [P, NH], F32, sc)
            st1 = sb("st1", [P, 2, 8, NH], F32, sc)
            relb = sb("relb", [BUCKETS + 1, NH], F32, sc)
            relbB = sb("relbB", [BUCKETS + 1, NH, P], F32, sc)
            oneh = sb("oneh", [BUCKETS + 1, SKEW], F32, sc)
            cln = sb("cln", [P, 2, T], F32, sc)
        brow = sc1[:, :, :, :].rearrange("p a h n -> p (a h n)")[:, 0:NH * SKEW].rearrange("p (h n) -> p h n", h=NH)
        skew_dram = nc.dram_tensor("skew_rows", (P, NH, SKEW), F32).ap()
        with ExitStack() as sc:
            fH = sb("fH", [P, KF, T], F32R, sc)
            fL = sb("fL", [P, KF, T], F32R, sc)
        with ExitStack() as sc:
            ug = sb("ug", [P, GR, T], F32, sc)
            gt = sb("gt", [P, 2 * KD, T], F32, sc)
            vga = sb("vga", [P, 4, T], F32, sc)
            vv = sb("vv", [P, NT, P], F32, sc)
            qkT = sb("qkT", [P, 5, T], F32, sc)
            qiT = sb("qiT", [P, 3, T], F32, sc)
            rl = sb("rl", [P, 2, T], F32, sc)
            pT2 = sb("pT2", [P, NT, 4, P], F32, sc)
            wT = sb("wT", [P, GR, P], F32, sc)
            wukv = sb("wukv", [P, 2, 2 * P], F32, sc)
            gkv = sb("gkv", [P, 2 * P], F32, sc)
            gqk = sb("gqk", [P, 2, P], F32, sc)
            causal = sb("causal", [P, P], F32, sc)
            ck = sb("ck", [P, NT, 2 * P], F32, sc)
            widx = sb("widx", [P, NT, 4], F32, sc)
            cosin = sb("cosin", [P, 2, NT, NROT], F32, sc)
            st2 = sb("st2", [P, 96], F32, sc)
            posi = sb("posi", [P, NT], I32, sc)
            posf = sb("posf", [P, NT], F32, sc)
            invb = sb("invb", [P, NROT], F32, sc)
            m8 = sb("m8", [P, 8], F32, sc)
        pflat = pT2[:, :, :, :].rearrange("p a b c -> p (a b c)")
        gvb = pflat[:, 0:1024].rearrange("p (a n) -> p a n", a=2)
        wsr = pflat[:, 1024:1536].rearrange("p (g n) -> p g n", g=GR)
        bsb = pflat[:, 1536:2048].rearrange("p (g n) -> p g n", g=GR)
        yflat = y[:, :, :].rearrange("p a b -> p (a b)")
        qk = yflat[:, 0:NT * 5 * P].rearrange("p (t h d) -> p t h d", t=NT, h=5)
        qi = yflat[:, NT * 5 * P:NT * 5 * P + NT * 6 * HD].rearrange("p (t h d) -> p t h d", t=NT, h=6)
        isc, madd = xn[:, 0, :], xn[:, 1, :]
        cnT = sq

        def rt_angle(f):
            return rt[:, f * P:f * P + NT * NROT]

        css, kss, vsum, vss = st2[:, 0:4], st2[:, 4:24], st2[:, 24:28], st2[:, 28:32]
        crs, krs, vrs, nmean = st2[:, 32:36], st2[:, 36:56], st2[:, 56:60], st2[:, 60:64]
        amax, ansum, arec = st2[:, 64:68], st2[:, 68:72], st2[:, 72:76]
        vmean = st2[:, 76:80]
        with ExitStack() as sc:
            skn = sb("skn", [P, 2 * PH, P], F32, sc)
            skT = sb("skT", [P, 2 * PH, P], F32, sc)
            qq = sb("qq", [P, 2, T], F32, sc)
            subs = sb("subs", [P, 4, NT, P], F32, sc)
            wk = sb("wk", [P, NT, 2 * P], F32, sc)
            cand = sb("cand", [P, NT, SEL, SEL], F32, sc)
            stop = sb("stop", [P, NT, 2 * PH, SEL], F32, sc)
            itop = sb("itop", [P, NT, 2 * PH, SEL], U32, sc)
            itf = sb("itf", [P, NT, 2 * PH, SEL], F32, sc)
            best = sb("best", [P, NT, PH, SEL], F32, sc)
            bpos = sb("bpos", [P, NT, PH, SEL], U32, sc)
            bhalf = sb("bhalf", [P, 2, NT, PH, SEL], U32, sc)
            bhf = sb("bhf", [P, 2, NT, PH, SEL], F32, sc)
            hot = sb("hot", [P, HS, SEL], F32, sc)
            sel = sb("sel", [P, 3, NT, HS], F32, sc)
            iota16 = sb("iota16", [P, SEL], F32, sc)
            bsum = sb("bsum", [P, NT * PH], F32, sc)
        icol, jcol, gcol = sq[:, 0, :], sq[:, 1, :], rt
        stream_scope.close()
        with ExitStack() as sc:
            Gs = sb("Gs", [P, 2, NEXP, P], F32, sc)
            Am = sb("Am", [P, 2 * TOK4, P], F32, sc)
            Bm = sb("Bm", [P, 2 * TOK4, P], F32, sc)
            iota128 = sb("iota128", [P, P], F32, sc)
        gd = nc.dram_tensor("gate_matrices", (NT, NEXP, P, P), F32).ap()
        with ExitStack() as sc:
            uraw = sb("uraw", [P, EG, D], F32, sc)
            vraw = sb("vraw", [P, EG, D], F32, sc)
            UH = sb("UH", [P, 2, KD, P], F32R, sc)
            UL = sb("UL", [P, 2, KD, P], F32R, sc)
            VH = sb("VH", [P, EG, D], F32R, sc)
            VL = sb("VL", [P, EG, D], F32R, sc)
            gr = sb("gr", [P, EG, T], F32, sc)
            ac = sb("ac", [P, 2, T], F32, sc)
            ga = sb("ga", [P, 2, T], F32, sc)
            GH = sb("GH", [P, EG, T], F32R, sc)
            GL = sb("GL", [P, EG, T], F32R, sc)
            o_nat = sb("o_nat", [P, NT * D], F32, sc)
        o_sb = o_nat[:, :] if STOP > 2 else yflat
        LAST = NGRP - 1
        block = ctx.enter_context(nc.Block())

        @block.tensor
        def _(pe):
            taken = [0]

            def take(*key):
                n = taken[0]
                taken[0] += 1
                number[key] = n
                if n >= 8:
                    pe.wait_ge(s(f"free{n % 8}"), n // 8)
                return banks[n % 8]

            def full(last, *key):
                last.then_inc(s(f"full{number[key] % 8}"), 1)

            def split(out, wh, wl, xh, xl, first, last, begins=False):
                mm = pe.matmul(out, wh, xh, start=first, stop=False)
                if begins:
                    mm.then_inc(s("w_begun"), 1)
                pe.matmul(out, wh, xl, start=False, stop=False)
                return pe.matmul(out, wl, xh, start=False, stop=last)

            def unit_views(key):
                u = unit_at[key]
                k, n, _ = units[u]
                pe.wait_ge(s("w_lo"), u + 1)
                return [w[:, u % NW, 0:k * n].rearrange("p (k n) -> p k n", k=k) for w in (WH, WL)]

            def project(key, out, k0=0, col=0, first=True, last=True, x0=0, ready=None):
                wh, wl = unit_views(key)
                n = units[unit_at[key]][0]
                for k in range(n):
                    if ready:
                        pe.wait_ge(s(ready[0]), ready[1] + k + 1)
                    mm = split(out, wh[:, k, col:col + P], wl[:, k, col:col + P], XH[:, x0 + k, :], XL[:, x0 + k, :],
                               first and k == 0, last and k == n - 1, begins=k == 0 and col == 0)
                return mm

            def tile(unit_key, key, **kw):
                out = take(*key)
                full(project(unit_key, out[:, :], **kw), *key)

            def square_sum(m, chunks=KD):
                take("ss", m)
                for k in range(chunks):
                    add_square(m, k, chunks)

            def add_square(m, k, chunks=KD):
                pe.wait_ge(s("squares"), squares_before[m] + k + 1)
                mm = pe.matmul(bank_of(("ss", m))[:, :], ones[:, :], sq[:, k % RING, :], start=k == 0,
                               stop=k == chunks - 1)
                if k < chunks - 1:
                    mm.then_inc(s("squares_used"), 1)
                else:
                    full(mm, "ss", m)

            def prepare():
                pe.wait_ge(s("ident_made"), 2)
                pe.wait_ge(s("vrows_landed"), 16 * len(VROWS))
                pe.wait_ge(s("ones_made"), 2)
                out = take("vec", 0)
                full(pe.transpose(out[:, 0:NV], vrows[0:NV, :], ident[0:NV, 0:NV]), "vec", 0)
                pe.wait_ge(s("taps_landed"), 16)
                out = take("vec", 1)
                n = TAPS * CC
                full(pe.transpose(out[:, 0:n], dwrows[0:n, :], ident[0:n, 0:n]), "vec", 1)
                for t in range(NT):
                    pe.wait_ge(s(f"x_landed{t}"), 16)
                for k in range(KD):
                    out = take("xT", k)
                    for t in range(NT):
                        mm = pe.transpose(out[:, t * P:(t + 1) * P], x_nat[:, t, k * P:(k + 1) * P], ident[:, :])
                    full(mm, "xT", k)
                square_sum(0)
                pe.wait_ge(s("relb_spread"), 1)
                for h in range(NH):
                    out = take("brow", h)
                    full(pe.matmul(out[:, 0:SKEW], relbB[:, h, :], oneh[:, :], start=True, stop=True), "brow", h)

            def first_projections():
                for c in range(CC):
                    tile(("cg", c), ("cg", c), ready=("x_lo", 0) if c == 0 else None)
                    tile(("ca", c), ("ca", c))
                for kv in range(2):
                    tile(("kk", kv), ("kk", kv))
                out = take("v", 0)
                wh, wl = unit_views(("v", 0))
                for t in range(NT):
                    for k in range(KD):
                        mm = split(out[:, t * P:(t + 1) * P], XH[:, k, t * P:(t + 1) * P], XL[:, k, t * P:(t + 1) * P],
                                   wh[:, k, :], wl[:, k, :], k == 0, k == KD - 1, begins=t == k == 0)
                full(mm, "v", 0)
                for c in range(4):
                    tile(("q", c), ("q", c))

            def scores(b):
                if b == 0:
                    for key in (("kk", 0), ("kk", 1), ("v", 0)) + tuple(("q", c) for c in range(4)):
                        wait_read(pe, key)
                w = P if b == 0 else 2 * P
                k0 = max(b - 1, 0) * P
                per = 512 // w
                for i in range(NH // per):
                    out = take("sc", b, i)
                    for j in range(per):
                        h = heads_of(i, per).start + 2 * j
                        half = slice((h % 2) * HD, (h % 2) * HD + HD)
                        mm = pe.matmul(out[:, j * w:(j + 1) * w], q1[half, h // 2, b * P:(b + 1) * P],
                                       kk[half, h // 4, k0:k0 + w], start=True, stop=True)
                    full(mm, "sc", b, i)

            def weighted_values(b):
                kts = [1] if b == 0 else [0, 1]
                pe.wait_ge(s("probs"), b + 1)
                for i in range(NH // 2):
                    out = take("pT", b, i)
                    for j in range(2):
                        for kt in kts:
                            w = (kt if b else 0) * P
                            mm = pe.transpose(out[:, (2 * j + kt) * P:(2 * j + kt + 1) * P],
                                              sc1[:, b % 2, 2 * i + j, w:w + P], ident[:, :])
                    full(mm, "pT", b, i)
                out = take("o", b)
                for h in range(NH):
                    if h % 2 == 0:
                        wait_read(pe, ("pT", b, h // 2))
                    half = slice((h % 2) * HD, (h % 2) * HD + HD)
                    kv = slice((h // 4) * HD, (h // 4) * HD + HD)
                    for kt in kts:
                        mm = pe.matmul(out[half, (h // 2) * P:(h // 2 + 1) * P], v1[:, b - 1 + kt, kv],
                                       pT1[:, h, kt, :], start=kt == kts[0], stop=kt == 1)
                full(mm, "o", b)

            def attention():
                scores(0)
                for b in range(NT):
                    if b + 1 < NT:
                        scores(b + 1)
                    weighted_values(b)

            def conv_tail():
                out = take("cmean", 0)
                for c in range(CC):
                    pe.wait_ge(s("conv_done"), c + 1)
                    mm = pe.matmul(out[:, :], ones[:, :], cacc[:, c, :], start=c == 0, stop=c == CC - 1)
                full(mm, "cmean", 0)
                square_sum(1, CC)
                for c in range(2):
                    for j in range(2):
                        out = take("pw", 2 * c + j)
                        mm = project(("pw", c), out[:, :], col=j * P, x0=4,
                                     ready=("conv_lo", 0) if c == j == 0 else None)
                        full(mm, "pw", 2 * c + j)

            def mix_out():
                for key in [("o", b) for b in range(NT)] + [("pw", c) for c in range(CC)]:
                    wait_read(pe, key)
                for c in range(KD):
                    tile(("wo", c), ("y", 0, c))
                    if c == 0:
                        take("ss", 2)
                    else:
                        add_square(2, c - 1)
                add_square(2, KD - 1)
                square_sum(3)

            def feed_forward():
                for c in range(KF):
                    tile(("wg", c), ("fg", c), ready=("x_lo", KD) if c == 0 else None)
                    tile(("wu", c), ("fu", c))
                for c in range(KD):
                    out = take("y", 1, c)
                    for j, (k0, k1) in enumerate(DOWN):
                        wh, wl = unit_views(("wd", c, j))
                        for k in range(k0, k1):
                            if c == 0:
                                pe.wait_ge(s("f_lo"), k + 1)
                            mm = split(out[:, :], wh[:, k - k0, :], wl[:, k - k0, :], fH[:, k, :], fL[:, k, :], k == 0,
                                       k == KF - 1, begins=k == k0)
                    full(mm, "y", 1, c)
                    if c == 0:
                        take("ss", 4)
                    else:
                        add_square(4, c - 1)
                add_square(4, KD - 1)
                if STOP > 1:
                    square_sum(5)

            def store_out(src, signal):
                for t in range(NT):
                    for half in range(2):
                        out = take("out", t, half)
                        if t == half == 0:
                            signal(pe)
                        for k in range(4):
                            mm = pe.transpose(out[:, k * P:(k + 1) * P], src[:, half * 4 + k, t * P:(t + 1) * P],
                                              ident[:, :])
                        full(mm, "out", t, half)

            def natural(name, key0):
                outs = [take(name, t) for t in range(NT)]
                for j in range(4):
                    wh, wl = unit_views((name, j))
                    for t in range(NT):
                        tok = slice(t * P, (t + 1) * P)
                        for i in range(2):
                            k = 2 * j + i
                            mm = split(outs[t][:, :], XH[:, k, tok], XL[:, k, tok], wh[:, i, :], wl[:, i, :], k == 0,
                                       k == KD - 1, begins=t == i == 0)
                        if j == 3:
                            full(mm, name, t)

            def second_projections():
                for c in range(4):
                    tile(("u2", c), ("u2", c), ready=("x_lo", 2 * KD) if c == 0 else None)
                natural("ci", 1536)
                out = take("kw", 0)
                wh, wl = unit_views(("kw", 0))
                for t in range(NT):
                    for k in range(KD):
                        mm = split(out[:, t * 68:(t + 1) * 68], XH[:, k, t * P:(t + 1) * P], XL[:, k, t * P:(t + 1) * P],
                                   wh[:, k, :], wl[:, k, :], k == 0, k == KD - 1, begins=t == k == 0)
                full(mm, "kw", 0)
                natural("qn", 1024)
                pe.wait_ge(s("cn_made"), NT)
                for j in range(2):
                    out = take("cT", j)
                    for t in range(NT):
                        mm = pe.transpose(out[:, t * P:(t + 1) * P], ck[:, t, j * P:(j + 1) * P], ident[:, :])
                    full(mm, "cT", j)
                natural("vn", 512)
                pe.wait_ge(s("wukv_landed"), 32)
                for i in range(2):
                    out = take("kv", i)
                    for t in (2 * i, 2 * i + 1):
                        for j in range(2):
                            if i == 0:
                                wait_read(pe, ("cT", j))
                            mm = pe.matmul(out[:, (t % 2) * 256:(t % 2) * 256 + 256], cnT[:, j, t * P:(t + 1) * P],
                                           wukv[:, j, :], start=j == 0, stop=j == 1)
                    full(mm, "kv", i)

            def second_transposes():
                pe.wait_ge(s("spatial_masked"), 1)
                out = take("wT", 0)
                for g in range(GR):
                    mm = pe.transpose(out[:, g * P:(g + 1) * P], wsr[:, g, :], ident[:, :])
                full(mm, "wT", 0)
                wait_read(pe, ("wT", 0))
                for t in range(NT):
                    pe.wait_ge(s("v_normed"), t + 1)
                    out = take("z", t)
                    for g in range(GR):
                        mm = pe.matmul(out[:, g * P:(g + 1) * P], vga[:, t, g * P:(g + 1) * P], wT[:, g, :],
                                       start=True, stop=True)
                    full(mm, "z", t)
                pe.wait_ge(s("rotated"), 2)
                for h in range(3):
                    out = take("iT", h)
                    for t in range(NT):
                        mm = pe.transpose(out[:, t * P:(t + 1) * P],
                                          qi[:, t, 2 * h:2 * h + 2, :].rearrange("p h d -> p (h d)"), ident[:, :])
                    full(mm, "iT", h)
                for h in range(5):
                    out = take("hT", h)
                    for t in range(NT):
                        mm = pe.transpose(out[:, t * P:(t + 1) * P], qk[:, t, h, :], ident[:, :])
                    full(mm, "hT", h)

            def sparse_attention():
                for b in range(NT):
                    n = (b + 1) * P
                    tok = slice(b * P, (b + 1) * P)
                    if b == 0:
                        for h in range(3):
                            wait_read(pe, ("iT", h))
                        for h in range(5):
                            wait_read(pe, ("hT", h))
                    for h in range(4):
                        out = take("ix", b, h)
                        half = slice((h % 2) * HD, (h % 2) * HD + HD)
                        full(pe.matmul(out[:, 0:n], qiT[half, h // 2, tok], qiT[half, 2, 0:n], start=True, stop=True),
                             "ix", b, h)
                    for h in range(4):
                        out = take("at", b, h)
                        full(pe.matmul(out[:, 0:n], qkT[:, h, tok], qkT[:, 4, 0:n], start=True, stop=True), "at", b, h)
                    for c in range(4):
                        tile(("gt", 4 * b + c), ("gt", 4 * b + c))
                    pe.wait_ge(s("probs2"), b + 1)
                    for kt in range(b + 1):
                        out = take("pT2", b, kt)
                        for h in range(4):
                            mm = pe.transpose(out[:, h * P:(h + 1) * P], vga[:, h, kt * P:(kt + 1) * P], ident[:, :])
                        full(mm, "pT2", b, kt)
                    out = take("yb", b)
                    for kt in range(b + 1):
                        wait_read(pe, ("pT2", b, kt))
                        mm = pe.matmul(out[:, :], vv[:, kt, :], pT2[:, kt, :, :].rearrange("p h q -> p (h q)"),
                                       start=kt == 0, stop=kt == b)
                    full(mm, "yb", b)

            def merge_and_out():
                for u in range(KD // 2):
                    for j, name in enumerate(("wa", "wb")):
                        for c in (2 * u, 2 * u + 1):
                            out = take(name, c)
                            full(project((name, u), out[:, :], col=(c % 2) * P, x0=4 * j,
                                         ready=("branch_lo", 4 * j) if c == 0 else None), name, c)
                for c in range(KD):
                    tile(("wo2", c), ("o2", c), ready=("merged_lo", 0) if c == 0 else None)
                if STOP > 2:
                    square_sum(6)

            def choose_experts():
                pe.wait_ge(s("subkeys_landed"), 16)
                for q in range(4):
                    out = take("sk", q)
                    for r in range(4):
                        mm = pe.transpose(out[:, r * P:(r + 1) * P], skn[:, 4 * q + r, :], ident[:, :])
                    full(mm, "sk", q)

                def sub(hp):
                    wait_read(pe, ("q2", hp))
                    wait_read(pe, ("sk", hp // 4))
                    out = take("sub", hp)
                    for t in range(NT):
                        mm = pe.matmul(out[:, t * P:(t + 1) * P], qq[:, hp % 2, t * P:(t + 1) * P], skT[:, hp, :],
                                       start=True, stop=True)
                    full(mm, "sub", hp)

                for hp in range(2 * PH):
                    tile(("wq", hp), ("q2", hp), ready=("x_lo", 3 * KD) if hp == 0 else None)
                    if hp:
                        sub(hp - 1)
                sub(2 * PH - 1)
                for t in range(NT):
                    pe.wait_ge(s("selected"), t + 1)
                    out = take("sel", t)
                    for j in range(3):
                        mm = pe.transpose(out[:, j * P:(j + 1) * P], sel[:, j, t, :], ident[:, :])
                    full(mm, "sel", t)

            def gate_matrices():
                for n in range(taken[0] - 8, taken[0]):
                    pe.wait_ge(s(f"free{n % 8}"), n // 8 + 1)
                pe.sem_inc(s("g_full"), 2)
                for tt in range(NT):
                    with pe.Fori(0, P // (2 * TOK4)) as n:
                        for q in range(2):
                            four = n * 2 + (tt * P // TOK4 + q)
                            pe.wait_ge(s("one_hots"), four * TOK4 + TOK4)
                            pe.wait_ge(s("g_copied"), four + 1)
                            for r in range(TOK4):
                                mm = pe.matmul(banks[q][:, r * P:(r + 1) * P], Bm[:, q * TOK4 + r, :],
                                               Am[:, q * TOK4 + r, :], start=True, stop=True)
                            mm.then_inc(s("g_full"), 1)

            def experts():
                def turn(x, e):
                    pe.wait_ge(s(f"u_landed{e}"), (x - e) * 4 + 16)
                    for half in range(2):
                        pe.wait_ge(s("ut_lo"), x * 2 + half + 1)
                        for k in range(4):
                            mm = pe.transpose(banks[half][:, k * P:(k + 1) * P],
                                              uraw[:, e, (half * 4 + k) * P:(half * 4 + k + 1) * P], ident[:, :])
                        mm.then_inc(s("ut_full"), 1)

                def up(x, b):
                    pe.wait_ge(s("ut_lo"), x * 2 + 4)
                    pe.wait_ge(s("gelu"), x + 1)
                    for k in range(KD):
                        mm = split(banks[2 + b][:, :], UH[:, b, k, :], UL[:, b, k, :], XH[:, k, :], XL[:, k, :],
                                   k == 0, k == KD - 1)
                    mm.then_inc(s("up_full"), 1)

                def down(g):
                    pe.wait_ge(s("ga_lo"), g * EG + EG + 2)
                    pe.wait_ge(s("v_lo"), g * EG + EG)
                    for c in range(KD):
                        pe.wait_ge(s("added"), g * KD + c + 1)
                        for e in range(EG):
                            cols = slice(c * P, (c + 1) * P)
                            mm = split(banks[4 + c % 2][:, :], VH[:, e, cols], VL[:, e, cols], GH[:, e, :], GL[:, e, :],
                                       e == 0, e == EG - 1)
                        mm.then_inc(s("down_full"), 1)

                pe.wait_ge(s("g_copied"), T // TOK4 + 2)
                pe.sem_inc(s("up_full"), 2)
                pe.sem_inc(s("down_full"), 1)
                turn(0, 0)
                turn(1, 1)
                up(0, 0)
                with pe.Fori(0, LAST) as g:
                    for e in range(1, EG + 1):
                        x = g * EG + e
                        turn(x + 1, (e + 1) % EG)
                        up(x, e % 2)
                    down(g)
                for x in range(LAST * EG + 1, NEXP):
                    if x + 1 < NEXP:
                        turn(x + 1, (x + 1) % EG)
                    up(x, x % 2)
                down(LAST)

            prepare()
            first_projections()
            attention()
            conv_tail()
            mix_out()
            feed_forward()
            if STOP > 1:
                second_projections()
                second_transposes()
                sparse_attention()
                merge_and_out()
            if STOP > 2:
                choose_experts()
                gate_matrices()
                experts()
            store_out(hT, [lambda eng: eng.wait_ge(s("resid"), 2 * KD),
                           lambda eng: [wait_read(eng, ("o2", c)) for c in range(KD)],
                           lambda eng: eng.wait_ge(s("added"), NGRP * KD + 2)][STOP - 1])

        def store(eng):
            for t in range(NT):
                for half in range(2):
                    wait_read(eng, ("out", t, half))
                eng.dma_start(out[0, t * P:(t + 1) * P, :], o_sb[:, t * D:(t + 1) * D]).then_inc(
                    s("stored"), 16)
            eng.wait_ge(s("stored"), 16 * NT)

        @block.sync
        def _(sp):
            x = A["x"][0]
            for t in range(NT):
                sp.dma_start(x_nat[:, t, :], x[t * P:(t + 1) * P, :]).then_inc(s(f"x_landed{t}"), 16)
                if t == 0:
                    at = 0
                    for name, src, n in VROWS:
                        sp.dma_start(vrows[at:at + n, :], src.rearrange("(c p) -> c p", p=P)).then_inc(s("vrows_landed"), 16)
                        at += n
                    sp.dma_start(dwrows[0:TAPS * CC, :], A["conv_dw"].rearrange("w (c p) -> (w c) p", p=P)).then_inc(
                        s("taps_landed"), 16)
                    sp.dma_start(relb[0:BUCKETS, :], A["rel_bias"]).then_inc(s("relb_landed"), 16)
                    sp.dma_start(oneh[:, :], onehot_rows).then_inc(s("relb_landed"), 16)
                    sp.dma_start(sinkb[:, :], A["attn_sinks"].rearrange("(a h) -> a h", a=1).partition_broadcast(P)).then_inc(
                        s("sinks_landed"), 16)

            def stream(u):
                k, n, parts = units[u]
                if u >= NR:
                    sp.wait_ge(s("w_lo"), u - NR + 1)
                for col, src in parts:
                    dst = wraw[:, u % NR, 0:k * n].rearrange("p (k n) -> p k n", k=k)[:, :, col:col + src.shape[2]]
                    sp.dma_start(dst, src).then_inc(s(f"w_landed{u % NR}"), 16)

            for u in range(6):
                stream(u)
            for h in range(NH):
                wait_read(sp, ("brow", h))
            sp.dma_start(skew_dram, brow[:, :, :]).then_inc(s("skew_out"), 16)
            sp.wait_ge(s("skew_out"), 16)
            back = bass.AP(skew_dram.tensor, P - 1, [[NH * SKEW - 1, P], [SKEW, NH], [1, 2 * P]])
            sp.dma_start(biasT[:, :, :], back).then_inc(s("bias_landed"), 16)
            def second_inputs():
                wait_full(sp, ("y", 1, KD - 1))
                sp.dma_start(posi[:, :], A["positions_2"].rearrange("a (t p) -> p (a t)", p=P),
                             allow_slow_non_contiguous=True).then_inc(s("pos_landed"), 16)
                sp.dma_start(invb[:, :], inv_freq.partition_broadcast(P)).then_inc(s("pos_landed"), 16)
                for j, w in enumerate(("w_uk_2", "w_uv_2")):
                    sp.dma_start(wukv[:, :, j * P:(j + 1) * P], chunked(A[w][0])).then_inc(s("wukv_landed"), 16)
                sp.dma_start(gkv[:, :], A["kv_norm_g_2"].partition_broadcast(P)).then_inc(s("gains_landed"), 16)
                sp.dma_start(gqk[:, 0, :], A["q_norm_g_2"].partition_broadcast(P)).then_inc(s("gains_landed"), 16)
                sp.dma_start(gqk[:, 1, :], A["k_norm_g_2"].partition_broadcast(P)).then_inc(s("gains_landed"), 16)
                sp.dma_start(gvb[:, 0, :], A["v_norm_g_2"].partition_broadcast(P)).then_inc(s("gains_landed"), 16)
                sp.dma_start(gvb[:, 1, :], A["v_norm_b_2"].partition_broadcast(P)).then_inc(s("gains_landed"), 16)
                sp.dma_start(bsb[:, :, :], A["spatial_b_2"].partition_broadcast(P)).then_inc(s("gains_landed"), 16)
                sp.dma_start(wsr[:, :, :], A["spatial_w_2"][0].rearrange("g t s -> t g s")).then_inc(s("wsr_landed"), 16)

            for u in range(6, len(units)):
                if STOP > 1 and u == unit_at[("u2", 0)] + 2:
                    second_inputs()
                if STOP > 2 and u == unit_at[("wq", 0)] + 2:
                    for c in range(KD):
                        wait_read(sp, ("wa", c))
                        wait_read(sp, ("wb", c))
                    sp.wait_ge(s("merged"), KD)
                    sp.dma_start(skn[:, :, :], A["peer_subkeys_2"][0].rearrange("h a n d -> n (h a) d")).then_inc(
                        s("subkeys_landed"), 16)
                stream(u)

            def gates_out():
                for tt in range(NT):
                    sp.wait_ge(s("g_copied"), (tt + 1) * P // TOK4 + 2)
                    sp.dma_start(gd[tt].rearrange("i j t -> j i t"), Gs[:, tt % 2, :, :]).then_inc(s(f"g_out{tt}"), 16)

            def load_experts():
                u_rows = A["peer_u_2"][0].rearrange("(i j) d -> i j d", j=P)
                v_rows = A["peer_v_2"][0].rearrange("(i j) d -> i j d", j=P)
                gates = gd.rearrange("g i j t -> i j g t")
                for tt in range(NT):
                    sp.wait_ge(s(f"g_out{tt}"), 16)

                def load(x, e, first):
                    if not first:
                        sp.wait_ge(s("ut_full"), x * 2 - 2 * EG + 2)
                    sp.dma_start(uraw[:, e, :], at_row(u_rows, x)).then_inc(s(f"u_landed{e}"), 16)
                    if not first:
                        sp.wait_ge(s("ga_f"), x - EG + 3)
                    sp.dma_start(gr[:, e, :].rearrange("p (g t) -> p g t", g=NT), at_row(gates, x)).then_inc(
                        s(f"g_landed{e}"), 16)
                    if not first:
                        sp.wait_ge(s("v_lo"), x - EG + 1)
                    sp.dma_start(vraw[:, e, :], at_row(v_rows, x)).then_inc(s(f"v_landed{e}"), 16)

                def at_row(view, x):
                    return view[x] if type(x) is int else view[bass.ds(x, 1)].squeeze(0)

                for e in range(EG):
                    load(e, e, True)
                with sp.Fori(1, NGRP) as g:
                    for e in range(EG):
                        load(g * EG + e, e, False)

            if STOP > 2:
                gates_out()
                load_experts()
            store(sp)

        @block.gpsimd
        def _(pool):
            pool.memset(ones[:, :], 1.0).then_inc(s("ones_made"), 1)
            pool.memset(eps[:, :], EPS).then_inc(s("ones_made"), 1)
            pool.memset(ident[:, :], 0.0).then_inc(s("ident_made"), 1)
            pool.wait_ge(s("ident_made"), 1)
            pool.affine_select(out=ident[:, :], in_=ident[:, :], compare_op=ALU.not_equal, fill=1.0, base=0,
                               pattern=[[-1, P]], channel_multiplier=1).then_inc(s("ident_made"), 1)
            for u, (k, n, _) in enumerate(units):
                if STOP > 1 and u == unit_at[("ci", 0)]:
                    pool.wait_ge(s("wsr_landed"), 16)
                    pool.affine_select(out=wsr[:, :, :], in_=wsr[:, :, :], compare_op=ALU.is_ge, fill=0.0, base=0,
                                       pattern=[[0, GR], [-1, P]], channel_multiplier=1).then_inc(s("spatial_masked"), 1)
                    pool.memset(causal[:, :], 0.0).then_inc(s("causal_made"), 1)
                    pool.wait_ge(s("causal_made"), 1)
                    pool.affine_select(out=causal[:, :], in_=causal[:, :], compare_op=ALU.is_ge, fill=NEG, base=0,
                                       pattern=[[-1, P]], channel_multiplier=1).then_inc(s("causal_made"), 1)
                pool.wait_ge(s("w_hi"), u + 1)
                if u >= NW:
                    pool.wait_ge(s("w_begun"), u - NW + 2)
                m = k * n
                if STOP > 2 and u == unit_at[("wq", 0)] + 2:
                    for c in range(KD):
                        wait_read(pool, ("wb", c))
                    pool.wait_ge(s("merged"), KD)
                    pool.iota(iota16[:, :], pattern=[[1, SEL]], base=0, channel_multiplier=0,
                              allow_small_or_imprecise_dtypes=True).then_inc(s("iota_made"), 1)
                pool.tensor_tensor(WL[:, u % NW, 0:m], wraw[:, u % NR, 0:m], WH[:, u % NW, 0:m].bitcast(F32),
                                   ALU.subtract).then_inc(s("w_lo"), 1)

            if STOP > 2:
                for t in range(NT):
                    wait_full(pool, ("sel", t))
                pool.iota(iota128[:, :], pattern=[[1, P]], base=0, channel_multiplier=0,
                          allow_small_or_imprecise_dtypes=True).then_inc(s("iota_made"), 1)
                with pool.Fori(0, NGRP) as g:
                    for e in range(EG):
                        pool.wait_ge(s("v_hi"), g * EG + e + 1)
                        pool.tensor_tensor(VL[:, e, :], vraw[:, e, :], VH[:, e, :].bitcast(F32), ALU.subtract).then_inc(
                            s("v_lo"), 1)

        @block.scalar
        def _(act):
            cast = [0]
            arrived = [0] * NR

            def cast_to(key_or_u):
                u1 = key_or_u if type(key_or_u) is int else unit_at[key_or_u] + 1
                while cast[0] <= min(u1, len(units) - 1):
                    u = cast[0]
                    k, n, parts = units[u]
                    arrived[u % NR] += 16 * len(parts)
                    act.wait_ge(s(f"w_landed{u % NR}"), arrived[u % NR])
                    if u >= NW:
                        act.wait_ge(s("w_begun"), u - NW + 2)
                    act.activation(WH[:, u % NW, 0:k * n], wraw[:, u % NR, 0:k * n], ACT.Copy).then_inc(s("w_hi"), 1)
                    cast[0] += 1

            def root_mean(m, n=D):
                ss = wait_full(act, ("ss", m))
                act.activation(rt[:, :], ss[:, :], ACT.Sqrt, bias=eps[:, 0:1], scale=1.0 / n).then_inc(frees(("ss", m)), 1)

            def square(m, k, src, signal=None):
                if k >= RING:
                    act.wait_ge(s("squares_used"), squares_signalled[m] + k - RING + 1)
                act.activation(sq[:, k % RING, :], src, ACT.Square).then_inc(s("squares"), 1)

            def high_of_norm(n):
                for k in range(KD):
                    act.wait_ge(s("xn"), n * KD + k + 1)
                    act.activation(XH[:, k, :], xn[:, k % RING, :], ACT.Copy).then_inc(s("x_hi"), 1)

            def prepare():
                act.wait_ge(s("ones_made"), 2)
                cast_to(1)
                for k in range(KD):
                    src = wait_full(act, ("xT", k))
                    act.activation(hT[:, k, :], src[:, :], ACT.Copy).then_inc(frees(("xT", k)), 1)
                    wait_read(act, ("xT", k))
                    square(0, k, hT[:, k, :])
                root_mean(0)
                high_of_norm(0)
                for h in range(NH):
                    src = wait_full(act, ("brow", h))
                    act.activation(brow[:, h, :], src[:, 0:SKEW], ACT.Copy).then_inc(frees(("brow", h)), 1)

            def first_projections():
                for c in range(CC):
                    cast_to(("cg", c))
                    src = wait_full(act, ("cg", c))
                    if c >= 2:
                        wait_read(act, ("ca", c - 2))
                    act.activation(sg[:, c % 2, :], src[:, :], ACT.Sigmoid).then_inc(frees(("cg", c)), 1)
                    cast_to(("ca", c))
                for key, dst in [(("kk", 0), kk[:, 0, :]), (("kk", 1), kk[:, 1, :]),
                                 (("v", 0), v1[:, :, :].rearrange("p t n -> p (t n)"))] + [
                                     (("q", c), q1[:, c, :]) for c in range(4)]:
                    cast_to(key)
                    src = wait_full(act, key)
                    act.activation(dst, src[:, :], ACT.Copy).then_inc(frees(key), 1)

            def attention():
                for b in range(NT):
                    w = P if b == 0 else 2 * P
                    st = st1[:, b % 2]
                    act.wait_ge(s("sink_gap"), b + 1)
                    for h in range(NH):
                        act.activation(sc1[:, b % 2, h, 0:w], sc1[:, b % 2, h, 0:w], ACT.Exp, bias=st[:, 1, h:h + 1],
                                       accum_out=st[:, 2, h:h + 1])
                    act.activation(st[:, 4, :], st[:, 3, :], ACT.Exp).then_inc(s("exps"), 1)
                    for i in range(NH // 2):
                        src = wait_full(act, ("pT", b, i))
                        kt0 = 1 if b == 0 else 0
                        if b and i == 0:
                            wait_full(act, ("o", b - 1))
                        act.activation(pT1[:, 2 * i:2 * i + 2, kt0:2, :],
                                       src[:, :].rearrange("p (h t q) -> p h t q", h=2, t=2)[:, :, kt0:2, :],
                                       ACT.Copy).then_inc(frees(("pT", b, i)), 1)
                    src = wait_full(act, ("o", b))
                    act.activation(XH[:, 0:4, b * P:(b + 1) * P], src[:, :].rearrange("p (c q) -> p c q", c=4),
                                   ACT.Copy).then_inc(s("att_hi"), 1)

            def conv_tail():
                for c in range(CC):
                    act.wait_ge(s("centred"), c + 1)
                    square(1, c, cacc[:, c, :])
                root_mean(1, CC * P)
                for c in range(CC):
                    act.wait_ge(s("ln_scaled"), c + 1)
                    act.activation(cacc[:, c, :], cacc[:, c, :], ACT.Silu, bias=vcol("ln_b", c)).then_inc(s("conv_silu"), 1)
                for c in range(CC):
                    act.wait_ge(s("conv_silu"), c + 1)
                    act.activation(XH[:, 4 + c, :], cacc[:, c, :], ACT.Copy).then_inc(s("conv_hi"), 1)
                cast_to(("pw", 1))
                wait_full(act, ("pw", CC - 1))
                for c in range(CC):
                    src = wait_full(act, ("pw", c))
                    act.activation(XH[:, 4 + c, :], src[:, :], ACT.Copy).then_inc(s("pw_hi"), 1)

            def residual(j, m, unit_keys):
                for c in range(KD):
                    cast_to(unit_keys(c))
                    src = wait_full(act, ("y", j, c))
                    square(m, c, src[:, :])
                    act.activation(y[:, c, :], src[:, :], ACT.Copy).then_inc(frees(("y", j, c)), 1)
                root_mean(m)
                if STOP == 1 and j == 1:
                    return
                for c in range(KD):
                    act.wait_ge(s("resid"), j * KD + c + 1)
                    square(m + 1, c, hT[:, c, :])
                root_mean(m + 1)

            sil = y[:, 0:2, :]
            ff = y[:, 2:4, :]

            def feed_forward():
                high_of_norm(1)

                def high(c):
                    wait_read(act, ("fu", c))
                    act.activation(fH[:, c, :], ff[:, c % 2, :], ACT.Copy).then_inc(s("f_hi"), 1)

                for c in range(KF):
                    cast_to(("wg", c))
                    src = wait_full(act, ("fg", c))
                    if c >= 2:
                        wait_read(act, ("fu", c - 2))
                    act.activation(sil[:, c % 2, :], src[:, :], ACT.Silu).then_inc(frees(("fg", c)), 1)
                    cast_to(("wu", c))
                    if c >= 1:
                        high(c - 1)
                high(KF - 1)

            def store_out():
                for t in range(NT):
                    for half in range(2):
                        src = wait_full(act, ("out", t, half))
                        at = t * D + half * 512
                        act.activation(o_sb[:, at:at + 512], src[:, :], ACT.Copy).then_inc(frees(("out", t, half)), 1)

            def act_link(ins):
                act_links[0] += 1
                ins.then_inc(s("act_link"), 1)
                act.wait_ge(s("act_link"), act_links[0])

            act_links = [0]

            def root(dst, src, n, signal):
                act.activation(dst, src, ACT.Sqrt, bias=eps[:, 0:1], scale=1.0 / n).then_inc(s(signal), 1)

            def second_projections():
                high_of_norm(2)
                for f in range(2):
                    act.wait_ge(s("angles"), f + 1)
                    act.activation(cosin[:, f, :, :].rearrange("p t n -> p (t n)"), rt_angle(f), ACT.Sin).then_inc(
                        s("trig"), 1)
                for c in range(4):
                    cast_to(("u2", c))
                    src = wait_full(act, ("u2", c))
                    act.activation(ug[:, c, :], src[:, :], ACT.Gelu_apprx_tanh).then_inc(frees(("u2", c)), 1)
                cast_to(("ci", 3))
                for t in range(NT):
                    src = wait_full(act, ("ci", t))
                    act.activation(vga[:, t, 0:256], src[:, 0:256], ACT.Square, accum_out=css[:, t:t + 1])
                    act.activation(qi[:, t, 0:4, :], src[:, 256:512].rearrange("p (h d) -> p h d", h=4), ACT.Copy)
                    act.activation(ck[:, t, :], src[:, 0:256], ACT.Copy).then_inc(frees(("ci", t)), 1)
                wait_read(act, ("ci", NT - 1))
                root(crs, css, 256, "c_root")
                cast_to(("kw", 0))
                src = wait_full(act, ("kw", 0))
                kw = src[:, 0:NT * 68].rearrange("p (t n) -> p t n", t=NT)
                act.activation(qi[:, :, 4, :], kw[:, :, 0:64], ACT.Copy)
                act.activation(widx[:, :, :], kw[:, :, 64:68], ACT.Copy, scale=0.5).then_inc(frees(("kw", 0)), 1)
                cast_to(("qn", 3))
                for t in range(NT):
                    src = wait_full(act, ("qn", t))
                    act.activation(qk[:, t, 0:4, :], src[:, :].rearrange("p (h d) -> p h d", h=4), ACT.Copy).then_inc(
                        frees(("qn", t)), 1)
                for j in range(2):
                    src = wait_full(act, ("cT", j))
                    act.activation(cnT[:, j, :], src[:, :], ACT.Copy).then_inc(frees(("cT", j)), 1)
                cast_to(("vn", 3))
                act.wait_ge(s("rotated"), 1)
                for t in range(NT):
                    src = wait_full(act, ("vn", t))
                    act.activation(vga[:, t, :], src[:, :], ACT.Gelu_apprx_tanh, accum_out=vsum[:, t:t + 1]).then_inc(
                        frees(("vn", t)), 1)
                for i in range(2):
                    src = wait_full(act, ("kv", i))
                    kv = src[:, :].rearrange("p (t j n) -> p t j n", t=2, j=2)
                    act.activation(qk[:, 2 * i:2 * i + 2, 4, :], kv[:, :, 0, :], ACT.Copy)
                    act.activation(vv[:, 2 * i:2 * i + 2, :], kv[:, :, 1, :], ACT.Copy).then_inc(frees(("kv", i)), 1)
                act.wait_ge(s("v_mean"), 1)
                for t in range(NT):
                    act_link(act.activation(rl[:, t % 2, :], vga[:, t, :], ACT.Square, bias=nmean[:, t:t + 1],
                                            accum_out=vss[:, t:t + 1]))
                root(vrs, vss, T, "v_root")
                act.wait_ge(s("k_squares"), 1)
                root(krs, kss, P, "k_root")

            def second_transposes():
                src = wait_full(act, ("wT", 0))
                act.activation(wT[:, :, :], src[:, :].rearrange("p (g n) -> p g n", g=GR), ACT.Copy).then_inc(
                    frees(("wT", 0)), 1)
                for h in range(3):
                    src = wait_full(act, ("iT", h))
                    act.activation(qiT[:, h, :], src[:, :], ACT.Copy).then_inc(frees(("iT", h)), 1)
                for h in range(5):
                    src = wait_full(act, ("hT", h))
                    act.activation(qkT[:, h, :], src[:, :], ACT.Copy).then_inc(frees(("hT", h)), 1)

            def sparse_attention():
                for b in range(NT):
                    n = (b + 1) * P
                    for h in range(4):
                        src = wait_full(act, ("ix", b, h))
                        if 4 * b + h >= 2:
                            act.wait_ge(s("index_added"), 4 * b + h - 1)
                        act.activation(rl[:, h % 2, 0:n], src[:, 0:n], ACT.Relu, scale=HD ** -0.5).then_inc(
                            frees(("ix", b, h)), 1)
                    for c in range(4 * b, 4 * b + 4):
                        cast_to(("gt", c))
                        src = wait_full(act, ("gt", c))
                        act.activation(gt[:, c, :], src[:, :], ACT.Sigmoid).then_inc(frees(("gt", c)), 1)
                    act.wait_ge(s("amax"), b + 1)
                    for h in range(4):
                        last = act.activation(vga[:, h, 0:n], vga[:, h, 0:n], ACT.Exp, bias=amax[:, h:h + 1],
                                              accum_out=ansum[:, h:h + 1])
                    last.then_inc(s("exps2"), 1)
                    for kt in range(b + 1):
                        src = wait_full(act, ("pT2", b, kt))
                        if kt == 0 and b:
                            wait_full(act, ("yb", b - 1))
                        act.activation(pT2[:, kt, :, :].rearrange("p h q -> p (h q)"), src[:, :], ACT.Copy).then_inc(
                            frees(("pT2", b, kt)), 1)
                    src = wait_full(act, ("yb", b))
                    act.activation(qkT[:, 0:4, b * P:(b + 1) * P], src[:, :].rearrange("p (h q) -> p h q", h=4),
                                   ACT.Copy).then_inc(frees(("yb", b)), 1)

            def merge_and_out():
                wait_full(act, ("gt", 2 * KD - 1))
                act.wait_ge(s("gated_u"), NT)
                for c in range(4):
                    act.activation(XH[:, c, :], ug[:, c, :], ACT.Copy).then_inc(s("branch_hi"), 1)
                wait_read(act, ("yb", NT - 1))
                for c in range(4):
                    act.activation(XH[:, 4 + c, :], qkT[:, c, :], ACT.Copy).then_inc(s("branch_hi"), 1)
                cast_to(("wb", 3))
                wait_full(act, ("wb", KD - 1))
                for c in range(KD):
                    act.wait_ge(s("merged"), c + 1)
                    act.activation(XH[:, c, :], y[:, c, :], ACT.Copy).then_inc(s("merged_hi"), 1)
                for c in range(KD):
                    cast_to(("wo2", c))
                    if STOP > 2:
                        if c < RING:
                            wait_read(act, ("o2", c))
                            square(6, c, hT[:, c, :])
                if STOP > 2:
                    for c in range(RING, KD):
                        wait_read(act, ("o2", c))
                        square(6, c, hT[:, c, :])
                    root_mean(6)

            def choose_experts():
                high_of_norm(3)
                for q in range(4):
                    src = wait_full(act, ("sk", q))
                    act.activation(skT[:, 4 * q:4 * q + 4, :].rearrange("p a b -> p (a b)"), src[:, :], ACT.Copy).then_inc(
                        frees(("sk", q)), 1)

                def sub(hp):
                    src = wait_full(act, ("sub", hp))
                    if hp >= 4:
                        act.wait_ge(s("ranked"), hp - 3)
                    act.activation(subs[:, hp % 4, :, :].rearrange("p a b -> p (a b)"), src[:, :], ACT.Copy).then_inc(
                        frees(("sub", hp)), 1)

                for hp in range(2 * PH):
                    cast_to(("wq", hp))
                    src = wait_full(act, ("q2", hp))
                    if hp >= 2:
                        wait_full(act, ("sub", hp - 2))
                    act.activation(qq[:, hp % 2, :], src[:, :], ACT.Copy).then_inc(frees(("q2", hp)), 1)
                    if hp:
                        sub(hp - 1)
                sub(2 * PH - 1)
                act.wait_ge(s("best_less_max"), 1)
                flat = best[:, :, :, :].rearrange("p a b c -> p (a b c)")
                act.activation(flat, flat, ACT.Exp).then_inc(s("gate_exps"), 1)
                for t in range(NT):
                    src = wait_full(act, ("sel", t))
                    tok = slice(t * P, (t + 1) * P)
                    act.activation(icol[:, tok], src[:, 0:P], ACT.Copy)
                    act.activation(jcol[:, tok], src[:, P:2 * P], ACT.Copy)
                    act.activation(gcol[:, tok], src[:, 2 * P:3 * P], ACT.Copy).then_inc(frees(("sel", t)), 1)

            def gate_matrices():
                act.sem_inc(s("g_copied"), 2)
                for tt in range(NT):
                    if tt >= 2:
                        act.wait_ge(s(f"g_out{tt - 2}"), 16)
                    with act.Fori(0, P // (2 * TOK4)) as n:
                        for q in range(2):
                            four = n * 2 + (tt * P // TOK4 + q)
                            act.wait_ge(s("g_full"), four + 3)
                            act.activation(
                                Gs[:, tt % 2, :, bass.ds(n * (2 * TOK4) + q * TOK4, TOK4)].rearrange("p i t -> p t i"),
                                banks[q][:, :].rearrange("p (t i) -> p t i", t=TOK4), ACT.Copy).then_inc(
                                    s("g_copied"), 1)

            def experts():
                def high_u(x, b):
                    act.wait_ge(s("up_full"), x + 1)
                    for half in range(2):
                        act.wait_ge(s("ut_full"), x * 2 + half + 1)
                        act.activation(UH[:, b, half * 4:half * 4 + 4, :].rearrange("p a b -> p (a b)"),
                                       banks[half][:, :], ACT.Copy).then_inc(s("ut_hi"), 1)

                def high_v(x, e, g):
                    act.wait_ge(s(f"v_landed{e}"), g * 16 + 16)
                    act.wait_ge(s("down_full"), g * KD + 1)
                    act.activation(VH[:, e, :], vraw[:, e, :], ACT.Copy).then_inc(s("v_hi"), 1)

                def activate(x, b):
                    act.wait_ge(s("up_full"), x + 3)
                    act.wait_ge(s("ga_f"), x + 1)
                    act.activation(ac[:, b, :], banks[2 + b][:, :], ACT.Gelu_apprx_tanh).then_inc(s("gelu"), 1)

                def high_a(x, e, g):
                    act.wait_ge(s("ga_f"), x + 3)
                    act.wait_ge(s("down_full"), g * KD + 1)
                    act.activation(GH[:, e, :], ga[:, e % 2, :], ACT.Copy).then_inc(s("ga_hi"), 1)

                for tt in range(NT):
                    act.wait_ge(s(f"g_out{tt}"), 16)
                act.sem_inc(s("gelu"), 2)
                high_u(0, 0)
                high_u(1, 1)
                high_v(0, 0, 0)
                activate(0, 0)
                high_a(0, 0, 0)
                with act.Fori(0, LAST) as g:
                    for e in range(1, EG + 1):
                        x = g * EG + e
                        group = g if e < EG else g + 1
                        high_u(x + 1, (e + 1) % 2)
                        if e < EG:
                            high_v(x, e, group)
                            activate(x, e % 2)
                            high_a(x, e, group)
                        else:
                            activate(x, 0)
                            high_a(x, 0, group)
                            high_v(x, 0, group)
                for x in range(LAST * EG + 1, NEXP):
                    if x + 1 < NEXP:
                        high_u(x + 1, (x + 1) % 2)
                    high_v(x, x % EG, LAST)
                    activate(x, x % 2)
                    high_a(x, x % EG, LAST)

            prepare()
            first_projections()
            attention()
            conv_tail()
            residual(0, 2, lambda c: ("wo", c))
            feed_forward()
            residual(1, 4, lambda c: ("wd", c, 2))
            if STOP > 1:
                second_projections()
                second_transposes()
                sparse_attention()
                merge_and_out()
            if STOP > 2:
                choose_experts()
                gate_matrices()
                experts()
            store_out()

        @block.vector
        def _(dve):
            links = [0]

            def link(ins):
                links[0] += 1
                ins.then_inc(s("dve_link"), 1)
                dve.wait_ge(s("dve_link"), links[0])

            def inverse_root(m):
                wait_read(dve, ("ss", m))
                link(dve.reciprocal(rstd[:, :], rt[:, :]))

            def norm(n, m, gain):
                def low(k):
                    dve.wait_ge(s("x_hi"), n * KD + k + 1)
                    dve.tensor_tensor(XL[:, k, :], xn[:, k % RING, :], XH[:, k, :].bitcast(F32), ALU.subtract).then_inc(
                        s("x_lo"), 1)

                inverse_root(m)
                for k in range(KD):
                    if n * KD + k >= RING:
                        dve.wait_ge(s("x_lo"), n * KD + k - RING + 1)
                    dve.scalar_tensor_tensor(out=xn[:, k % RING, :], in0=hT[:, k, :], scalar=vcol(gain, k),
                                             in1=rstd[:, :], op0=ALU.mult, op1=ALU.mult).then_inc(s("xn"), 1)
                    if k >= 1:
                        low(k - 1)
                low(KD - 1)

            def prepare():
                dve.memset(hpad[:, :, 0:TAPS - 1], 0.0)
                dve.memset(relb[BUCKETS:BUCKETS + 1, :], NEG).then_inc(s("dve_link"), 1)
                links[0] += 1
                dve.wait_ge(s("dve_link"), links[0])
                dve.wait_ge(s("relb_landed"), 32)
                dve.tensor_copy(relbB[:, :, :], relb[:, :].unsqueeze(2).to_broadcast([BUCKETS + 1, NH, P])).then_inc(
                    s("relb_spread"), 1)
                src = wait_full(dve, ("vec", 0))
                dve.tensor_copy(vec[:, 0:NV], src[:, 0:NV]).then_inc(frees(("vec", 0)), 1)
                src = wait_full(dve, ("vec", 1))
                dve.tensor_copy(taps[:, 0:TAPS * CC], src[:, 0:TAPS * CC]).then_inc(frees(("vec", 1)), 1)
                wait_read(dve, ("vec", 0))
                wait_read(dve, ("vec", 1))
                norm(0, 0, "mix_pre")

            def convolution():
                for c in range(CC):
                    wait_read(dve, ("cg", c))
                    src = wait_full(dve, ("ca", c))
                    dve.tensor_tensor(hpad[:, c, TAPS - 1:], src[:, :], sg[:, c % 2, :], ALU.mult).then_inc(
                        frees(("ca", c)), 1)
                    wait_read(dve, ("ca", c))
                    link(dve.tensor_scalar(cacc[:, c, :], hpad[:, c, 0:T], taps[:, c:c + 1], vcol("dw_b", c),
                                           ALU.mult, ALU.add))
                    for w in range(1, TAPS):
                        step = dve.scalar_tensor_tensor(out=cacc[:, c, :], in0=hpad[:, c, w:w + T],
                                                        scalar=taps[:, w * CC + c:w * CC + c + 1], in1=cacc[:, c, :],
                                                        op0=ALU.mult, op1=ALU.add)
                        if w < TAPS - 1:
                            link(step)
                        else:
                            step.then_inc(s("conv_done"), 1)

            def attention():
                dve.wait_ge(s("bias_landed"), 16)
                dve.wait_ge(s("sinks_landed"), 16)

                def logits(b):
                    w = P if b == 0 else 2 * P
                    per = 512 // w
                    st = st1[:, b % 2]
                    for i in range(NH // per):
                        src = wait_full(dve, ("sc", b, i))
                        if b >= 2 and i == 0:
                            wait_full(dve, ("pT", b - 2, 3))
                        heads = heads_of(i, per)
                        dve.scalar_tensor_tensor(out=sc1[:, b % 2, heads, 0:w],
                                                 in0=src[:, :].rearrange("p (j w) -> p j w", w=w), scalar=HD ** -0.5,
                                                 in1=biasT[:, heads, 2 * P - w:2 * P],
                                                 op0=ALU.mult, op1=ALU.add).then_inc(frees(("sc", b, i)), 1)
                    wait_read(dve, ("sc", b, NH // per - 1))
                    link(dve.tensor_reduce(st[:, 0, :], sc1[:, b % 2, :, 0:w], AX_X, ALU.max))
                    link(dve.tensor_tensor(st[:, 0, :], st[:, 0, :], sinkb[:, :], ALU.max))
                    dve.tensor_scalar(st[:, 1, :], st[:, 0, :], -1.0, None, ALU.mult)
                    dve.tensor_tensor(st[:, 3, :], sinkb[:, :], st[:, 0, :], ALU.subtract).then_inc(s("sink_gap"), 1)

                def normalise(b):
                    w = P if b == 0 else 2 * P
                    st = st1[:, b % 2]
                    dve.wait_ge(s("exps"), b + 1)
                    link(dve.tensor_tensor(st[:, 5, :], st[:, 2, :], st[:, 4, :], ALU.add))
                    link(dve.reciprocal(st[:, 6, :], st[:, 5, :]))
                    pr = sc1[:, b % 2, :, 0:w]
                    dve.tensor_tensor(pr, pr, st[:, 6, :].unsqueeze(2).to_broadcast([P, NH, w]), ALU.mult).then_inc(
                        s("probs"), 1)

                def low(b):
                    dve.wait_ge(s("att_hi"), b + 1)
                    src = wait_full(dve, ("o", b))
                    to = slice(b * P, (b + 1) * P)
                    dve.tensor_tensor(XL[:, 0:4, to], src[:, :].rearrange("p (c q) -> p c q", c=4),
                                      XH[:, 0:4, to].bitcast(F32), ALU.subtract).then_inc(frees(("o", b)), 1)

                logits(0)
                for b in range(NT):
                    if b + 1 < NT:
                        logits(b + 1)
                    normalise(b)
                    if b:
                        low(b - 1)
                low(NT - 1)

            def conv_tail():
                src = wait_full(dve, ("cmean", 0))
                dve.tensor_scalar(cln[:, 0, :], src[:, :], 1.0 / (CC * P), None, ALU.mult).then_inc(frees(("cmean", 0)), 1)
                wait_read(dve, ("cmean", 0))
                for c in range(CC):
                    dve.tensor_tensor(cacc[:, c, :], cacc[:, c, :], cln[:, 0, :], ALU.subtract).then_inc(s("centred"), 1)
                inverse_root(1)
                for c in range(CC):
                    dve.scalar_tensor_tensor(out=cacc[:, c, :], in0=cacc[:, c, :], scalar=vcol("ln_g", c),
                                             in1=rstd[:, :], op0=ALU.mult, op1=ALU.mult).then_inc(s("ln_scaled"), 1)
                for c in range(CC):
                    dve.wait_ge(s("conv_hi"), c + 1)
                    dve.tensor_tensor(XL[:, 4 + c, :], cacc[:, c, :], XH[:, 4 + c, :].bitcast(F32), ALU.subtract).then_inc(
                        s("conv_lo"), 1)
                for c in range(CC):
                    dve.wait_ge(s("pw_hi"), c + 1)
                    src = wait_full(dve, ("pw", c))
                    dve.tensor_tensor(XL[:, 4 + c, :], src[:, :], XH[:, 4 + c, :].bitcast(F32), ALU.subtract).then_inc(
                        frees(("pw", c)), 1)

            def residual(j, m, gain):
                def add(c):
                    dve.wait_ge(s("y_scaled"), j * KD + c + 1)
                    dve.tensor_tensor(hT[:, c, :], hT[:, c, :], y[:, c, :], ALU.add).then_inc(s("resid"), 1)

                inverse_root(m)
                for c in range(KD):
                    dve.scalar_tensor_tensor(out=y[:, c, :], in0=y[:, c, :], scalar=vcol(gain, c), in1=rstd[:, :],
                                             op0=ALU.mult, op1=ALU.mult).then_inc(s("y_scaled"), 1)
                    if c:
                        add(c - 1)
                add(KD - 1)

            sil = y[:, 0:2, :]
            ff = y[:, 2:4, :]

            def feed_forward():
                def low(c):
                    dve.wait_ge(s("f_hi"), c + 1)
                    dve.tensor_tensor(fL[:, c, :], ff[:, c % 2, :], fH[:, c, :].bitcast(F32), ALU.subtract).then_inc(
                        s("f_lo"), 1)

                for c in range(KF):
                    wait_read(dve, ("fg", c))
                    src = wait_full(dve, ("fu", c))
                    if c >= 2:
                        dve.wait_ge(s("f_lo"), c - 1)
                    dve.tensor_tensor(ff[:, c % 2, :], src[:, :], sil[:, c % 2, :], ALU.mult).then_inc(frees(("fu", c)), 1)
                    if c:
                        low(c - 1)
                low(KF - 1)

            def angles():
                dve.wait_ge(s("pos_landed"), 32)
                link(dve.tensor_copy(posf[:, :], posi[:, :]))
                ang = rl[:, 0, 0:NT * NROT]
                turns = rl[:, 0, 128:128 + NT * NROT]
                link(dve.tensor_tensor(ang.rearrange("p (t n) -> p t n", t=NT),
                                       posf[:, :].unsqueeze(2).to_broadcast([P, NT, NROT]),
                                       invb[:, :].unsqueeze(1).to_broadcast([P, NT, NROT]), ALU.mult))
                for f in range(2):
                    quarter = 0.25 if f == 0 else 0.0
                    r = rt_angle(f)
                    link(dve.tensor_scalar(turns, ang, 1.0 / (2 * math.pi), quarter, ALU.mult, ALU.add))
                    link(dve.tensor_scalar(turns, turns, ROUND, -ROUND, ALU.add, ALU.add))
                    link(dve.scalar_tensor_tensor(out=r, in0=turns, scalar=-TURN[0], in1=ang, op0=ALU.mult, op1=ALU.add))
                    for part in TURN[1:]:
                        link(dve.scalar_tensor_tensor(out=r, in0=turns, scalar=-part, in1=r, op0=ALU.mult, op1=ALU.add))
                    link(dve.tensor_scalar(r, r, quarter * 2 * math.pi, PI_BELOW, ALU.add, ALU.min))
                    dve.tensor_scalar(r, r, -PI_BELOW, None, ALU.max).then_inc(s("angles"), 1)

            def rotate(x, half, at, heads, signal=None):
                x1, x2 = x[:, :, 0:heads, 0:half], x[:, :, 0:heads, half:2 * half]
                c, sn = (cosin[:, f, :, at:at + half].unsqueeze(2).to_broadcast([P, NT, heads, half]) for f in range(2))
                n = NT * heads * half
                tmp = [vga[:, j, 0:n].rearrange("p (t h d) -> p t h d", t=NT, h=heads) for j in range(4)]
                dve.tensor_tensor(tmp[0], x1, c, ALU.mult)
                dve.tensor_tensor(tmp[1], x2, sn, ALU.mult)
                dve.tensor_tensor(tmp[2], x2, c, ALU.mult)
                link(dve.tensor_tensor(tmp[3], x1, sn, ALU.mult))
                dve.tensor_tensor(x1, tmp[0], tmp[1], ALU.subtract)
                last = dve.tensor_tensor(x2, tmp[2], tmp[3], ALU.add)
                last.then_inc(signal, 1) if signal else link(last)

            def second_projections():
                angles()
                dve.wait_ge(s("gains_landed"), 6 * 16)
                dve.wait_ge(s("c_root"), 1)
                link(dve.reciprocal(crs, crs))
                for t in range(NT):
                    dve.scalar_tensor_tensor(out=ck[:, t, :], in0=ck[:, t, :], scalar=crs[:, t:t + 1], in1=gkv[:, :],
                                             op0=ALU.mult, op1=ALU.mult).then_inc(s("cn_made"), 1)
                wait_read(dve, ("kw", 0))
                dve.wait_ge(s("trig"), 2)
                rotate(qi, 8, 16, 5)
                dve.tensor_copy(qi[:, :, 5, :], qi[:, :, 4, :]).then_inc(s("rotated"), 1)

            def second_norms():
                for t in range(NT):
                    wait_read(dve, ("vn", t))
                link(dve.tensor_scalar(vmean, vsum, 1.0 / T, None, ALU.mult))
                dve.tensor_scalar(nmean, vmean, -1.0, None, ALU.mult).then_inc(s("v_mean"), 1)
                dve.wait_ge(s("v_root"), 1)
                link(dve.reciprocal(vrs, vrs))
                for t in range(NT):
                    v = vga[:, t, :]
                    link(dve.tensor_scalar(v, v, vmean[:, t:t + 1], vrs[:, t:t + 1], ALU.subtract, ALU.mult))
                    link(dve.tensor_tensor(v, v, gvb[:, 0, :], ALU.mult))
                    dve.tensor_tensor(v, v, gvb[:, 1, :], ALU.add).then_inc(s("v_normed"), 1)
                for t in range(NT):
                    wait_read(dve, ("qn", t))
                for i in range(2):
                    wait_read(dve, ("kv", i))
                for t in range(NT):
                    sqs = gt[:, 8 + 2 * t:8 + 2 * t + 2, :].rearrange("p a b -> p (a b)")[:, 0:5 * P].rearrange(
                        "p (h d) -> p h d", h=5)
                    link(dve.tensor_tensor(sqs, qk[:, t, :, :], qk[:, t, :, :], ALU.mult))
                    last = dve.tensor_reduce(kss[:, 5 * t:5 * t + 5], sqs, AX_X, ALU.add)
                last.then_inc(s("k_squares"), 1)
                dve.wait_ge(s("k_root"), 1)
                link(dve.reciprocal(krs, krs))
                for t in range(NT):
                    x = qk[:, t, :, :]
                    link(dve.tensor_tensor(x, x, krs[:, 5 * t:5 * t + 5].unsqueeze(2).to_broadcast([P, 5, P]), ALU.mult))
                    dve.tensor_tensor(x[:, 0:4, :], x[:, 0:4, :], gqk[:, 0:1, :].to_broadcast([P, 4, P]), ALU.mult)
                    link(dve.tensor_tensor(x[:, 4, :], x[:, 4, :], gqk[:, 1, :], ALU.mult))
                for t in range(NT):
                    src = wait_full(dve, ("z", t))
                    tok = slice(t * P, (t + 1) * P)
                    z = gt[:, 8 + t, :].rearrange("p (g n) -> p g n", g=GR)
                    dve.tensor_tensor(z, src[:, :].rearrange("p (g n) -> p g n", g=GR), bsb[:, :, :], ALU.add).then_inc(
                        frees(("z", t)), 1)
                    wait_read(dve, ("z", t))
                    dve.tensor_tensor(ug[:, :, tok], ug[:, :, tok], z, ALU.mult).then_inc(s("gated_u"), 1)
                dve.wait_ge(s("gated_u"), NT)
                rotate(qk, 16, 0, 5, s("rotated"))

            def sparse_attention():
                for b in range(NT):
                    n = (b + 1) * P
                    sc = isc[:, 0:n]
                    for h in range(4):
                        wait_read(dve, ("ix", b, h))
                        w = widx[:, b, h:h + 1]
                        if h == 0:
                            add = dve.tensor_scalar(sc, rl[:, 0, 0:n], w, None, ALU.mult)
                        else:
                            dve.wait_ge(s("index_added"), 4 * b + h)
                            add = dve.scalar_tensor_tensor(out=sc, in0=rl[:, h % 2, 0:n], scalar=w, in1=sc,
                                                           op0=ALU.mult, op1=ALU.add)
                        add.then_inc(s("index_added"), 1)
                    dve.wait_ge(s("index_added"), 4 * b + 4)
                    if b == 0:
                        dve.wait_ge(s("causal_made"), 2)
                        link(dve.tensor_copy(madd[:, 0:n], causal[:, :]))
                    else:
                        link(dve.tensor_tensor(sc[:, b * P:n], sc[:, b * P:n], causal[:, :], ALU.add))
                        for _ in range(TOPK // 8):
                            link(dve.max(m8[:, :], sc))
                            link(dve.match_replace(out=sc, in_to_replace=m8[:, :], in_values=sc, imm_value=TAKEN))
                        link(dve.tensor_scalar(madd[:, 0:n], sc, TAKEN / 2, NEG, ALU.is_gt, ALU.mult))
                    for h in range(4):
                        src = wait_full(dve, ("at", b, h))
                        dve.scalar_tensor_tensor(out=vga[:, h, 0:n], in0=src[:, 0:n], scalar=P ** -0.5,
                                                 in1=madd[:, 0:n], op0=ALU.mult, op1=ALU.add).then_inc(
                                                     frees(("at", b, h)), 1)
                    for h in range(4):
                        wait_read(dve, ("at", b, h))
                    link(dve.tensor_reduce(amax, vga[:, :, 0:n], AX_X, ALU.max))
                    dve.tensor_scalar(amax, amax, -1.0, None, ALU.mult).then_inc(s("amax"), 1)
                    dve.wait_ge(s("exps2"), b + 1)
                    link(dve.reciprocal(arec, ansum))
                    dve.tensor_tensor(vga[:, :, 0:n], vga[:, :, 0:n], arec.unsqueeze(2).to_broadcast([P, 4, n]),
                                      ALU.mult).then_inc(s("probs2"), 1)

            def merge_and_out():
                for c in range(KD):
                    src = ug[:, c, :] if c < 4 else qkT[:, c - 4, :]
                    dve.wait_ge(s("branch_hi"), c + 1)
                    dve.tensor_tensor(XL[:, c, :], src, XH[:, c, :].bitcast(F32), ALU.subtract).then_inc(
                        s("branch_lo"), 1)
                for c in range(KD):
                    wait_read(dve, ("gt", c))
                    wait_read(dve, ("gt", KD + c))
                    src = wait_full(dve, ("wa", c))
                    dve.tensor_tensor(y[:, c, :], src[:, :], gt[:, c, :], ALU.mult).then_inc(frees(("wa", c)), 1)
                    src = wait_full(dve, ("wb", c))
                    dve.tensor_tensor(gt[:, KD + c, :], src[:, :], gt[:, KD + c, :], ALU.mult).then_inc(
                        frees(("wb", c)), 1)
                    wait_read(dve, ("wa", c))
                    wait_read(dve, ("wb", c))
                    dve.tensor_tensor(y[:, c, :], y[:, c, :], gt[:, KD + c, :], ALU.add).then_inc(s("merged"), 1)
                for c in range(KD):
                    dve.wait_ge(s("merged_hi"), c + 1)
                    dve.tensor_tensor(XL[:, c, :], y[:, c, :], XH[:, c, :].bitcast(F32), ALU.subtract).then_inc(
                        s("merged_lo"), 1)
                for c in range(KD):
                    src = wait_full(dve, ("o2", c))
                    dve.tensor_tensor(hT[:, c, :], hT[:, c, :], src[:, :], ALU.add).then_inc(frees(("o2", c)), 1)

            def best16(src, work, values, indices, stages):
                for t in range(NT):
                    last = dve.max(values(t, 0), src(t))
                link(last)
                for t in range(NT):
                    dve.max_index(indices(t, 0), values(t, 0), src(t))
                    last = dve.match_replace(out=work(t), in_to_replace=values(t, 0), in_values=src(t), imm_value=TAKEN)
                link(last)
                for t in range(NT):
                    last = dve.max(values(t, 1), work(t))
                link(last)
                for t in range(NT):
                    last = dve.max_index(indices(t, 1), values(t, 1), work(t))
                return last

            def choose_experts():
                norm(3, 6, "norm2")
                for hp in range(2 * PH):
                    wait_read(dve, ("sub", hp))
                    best16(lambda t: subs[:, hp % 4, t, :], lambda t: wk[:, t, 0:P],
                           lambda t, i: stop[:, t, hp, 8 * i:8 * i + 8], lambda t, i: itop[:, t, hp, 8 * i:8 * i + 8],
                           0).then_inc(s("ranked"), 1)
                    dve.wait_ge(s("ranked"), hp + 1)
                    if hp % 2:
                        h = hp // 2
                        link(dve.tensor_tensor(cand[:, :, :, :],
                                               stop[:, :, hp - 1, :].unsqueeze(3).to_broadcast([P, NT, SEL, SEL]),
                                               stop[:, :, hp, :].unsqueeze(2).to_broadcast([P, NT, SEL, SEL]), ALU.add))
                        link(best16(lambda t: cand[:, t, :, :].rearrange("p a b -> p (a b)"), lambda t: wk[:, t, :],
                                    lambda t, i: best[:, t, h, 8 * i:8 * i + 8],
                                    lambda t, i: bpos[:, t, h, 8 * i:8 * i + 8], 0))
                b3 = best[:, :, :, :].rearrange("p t h s -> p (t h) s")
                link(dve.tensor_copy(bsum[:, :], b3[:, :, 0]))
                dve.tensor_tensor(b3, b3, bsum[:, :].unsqueeze(2).to_broadcast([P, NT * PH, SEL]),
                                  ALU.subtract).then_inc(s("best_less_max"), 1)
                p4 = bpos[:, :, :, :]
                dve.tensor_scalar(bhalf[:, 0, :, :, :], p4, 4, None, ALU.logical_shift_right)
                dve.tensor_scalar(bhalf[:, 1, :, :, :], p4, SEL - 1, None, ALU.bitwise_and)
                link(dve.tensor_copy(itf[:, :, :, :], itop[:, :, :, :]))
                link(dve.tensor_copy(bhf[:, :, :, :, :].rearrange("p a t h s -> p (a t h s)"),
                                     bhalf[:, :, :, :, :].rearrange("p a t h s -> p (a t h s)")))
                dve.wait_ge(s("gate_exps"), 1)
                link(dve.tensor_reduce(bsum[:, :], b3, AX_X, ALU.add))
                link(dve.reciprocal(bsum[:, :], bsum[:, :]))
                link(dve.tensor_tensor(sel[:, 2, :, :].rearrange("p t (h s) -> p (t h) s", h=PH), b3,
                                       bsum[:, :].unsqueeze(2).to_broadcast([P, NT * PH, SEL]), ALU.mult))
                dve.wait_ge(s("iota_made"), 1)
                for t in range(NT):
                    for part in range(2):
                        rank = bhf[:, part, t, :, :].rearrange("p h s -> p (h s)")
                        link(dve.tensor_tensor(hot[:, :, :], rank.unsqueeze(2).to_broadcast([P, HS, SEL]),
                                               iota16[:, :].unsqueeze(1).to_broadcast([P, HS, SEL]), ALU.is_equal))
                        h4 = hot[:, :, :].rearrange("p (h s) a -> p h s a", h=PH)
                        link(dve.tensor_tensor(h4, h4, itf[:, t, part::2, :].unsqueeze(2).to_broadcast(
                            [P, PH, SEL, SEL]), ALU.mult))
                        last = dve.tensor_reduce(sel[:, part, t, :], hot[:, :, :], AX_X, ALU.add)
                        if part == 0:
                            link(last)
                    last.then_inc(s("selected"), 1)
                    dve.wait_ge(s("selected"), t + 1)

            def gate_matrices():
                dve.wait_ge(s("iota_made"), 2)
                for t in range(NT):
                    wait_read(dve, ("sel", t))
                for tt in range(NT):
                    with dve.Fori(0, P // (2 * TOK4)) as n:
                        for q in range(2):
                            four = n * 2 + (tt * P // TOK4 + q)
                            dve.wait_ge(s("g_full"), four + 1)
                            for r in range(TOK4):
                                col = bass.ds(n * (2 * TOK4) + (tt * P + q * TOK4 + r), 1)
                                dve.tensor_scalar(Bm[:, q * TOK4 + r, :], iota128[:, :], jcol[:, col], None,
                                                  ALU.is_equal)
                                dve.tensor_scalar(Am[:, q * TOK4 + r, :], iota128[:, :], icol[:, col], gcol[:, col],
                                                  ALU.is_equal, ALU.mult).then_inc(s("one_hots"), 1)

            def experts():
                def low_u(x, b):
                    for half in range(2):
                        dve.wait_ge(s("ut_hi"), x * 2 + half + 1)
                        to = [w[:, b, half * 4:half * 4 + 4, :].rearrange("p a b -> p (a b)") for w in (UL, UH)]
                        dve.tensor_tensor(to[0], banks[half][:, :], to[1].bitcast(F32), ALU.subtract).then_inc(
                            s("ut_lo"), 1)

                def weigh(x, e, g):
                    dve.wait_ge(s("gelu"), x + 3)
                    dve.wait_ge(s(f"g_landed{e}"), g * 16 + 16)
                    dve.wait_ge(s("ga_lo"), x + 1)
                    dve.tensor_tensor(ga[:, e % 2, :], ac[:, e % 2, :], gr[:, e, :], ALU.mult).then_inc(s("ga_f"), 1)

                def low_a(x, e):
                    dve.wait_ge(s("ga_hi"), x + 1)
                    dve.tensor_tensor(GL[:, e, :], ga[:, e % 2, :], GH[:, e, :].bitcast(F32), ALU.subtract).then_inc(
                        s("ga_lo"), 1)

                def add(g):
                    for c in range(KD):
                        dve.wait_ge(s("down_full"), g * KD + c + 2)
                        dve.tensor_tensor(hT[:, c, :], hT[:, c, :], banks[4 + c % 2][:, :], ALU.add).then_inc(
                            s("added"), 1)

                for name in ("ut_lo", "ga_f", "ga_lo", "added"):
                    dve.sem_inc(s(name), 2)
                low_u(0, 0)
                low_u(1, 1)
                weigh(0, 0, 0)
                low_a(0, 0)
                with dve.Fori(0, LAST) as g:
                    for e in range(1, EG + 1):
                        x = g * EG + e
                        low_u(x + 1, (e + 1) % 2)
                        weigh(x, e % EG, g if e < EG else g + 1)
                        if e == EG:
                            add(g)
                        low_a(x, e % EG)
                for x in range(LAST * EG + 1, NEXP):
                    if x + 1 < NEXP:
                        low_u(x + 1, (x + 1) % 2)
                    weigh(x, x % EG, LAST)
                    low_a(x, x % EG)
                add(LAST)

            prepare()
            convolution()
            attention()
            conv_tail()
            residual(0, 2, "mix_post")
            norm(1, 3, "ffn_pre")
            feed_forward()
            residual(1, 4, "ffn_post")
            if STOP > 1:
                norm(2, 5, "norm1")
                second_projections()
                second_norms()
                sparse_attention()
                merge_and_out()
            if STOP > 2:
                choose_experts()
                gate_matrices()
                experts()


def kernel(**inputs):
    import numpy as _np
    import concourse.bacc as _bacc
    from concourse import mybir as _mybir
    from concourse.bass_utils import run_bass_kernel_spmd as _run

    nc = _bacc.Bacc("TRN2", target_bir_lowering=False, num_devices=1)
    onehot, inv = shape_constants()
    arrays, views = {}, {}
    for name, value in list(inputs.items()) + [("onehot_rows", onehot), ("inv_freq", inv)]:
        a = _np.ascontiguousarray(value)
        arrays[f"in_{name}"] = a
        views[name] = nc.dram_tensor(f"in_{name}", a.shape, _mybir.dt.from_np(a.dtype), kind="ExternalInput").ap()
    out = nc.dram_tensor("out", (1, T, D), F32, kind="ExternalOutput").ap()
    onehot_rows, inv_freq = views.pop("onehot_rows"), views.pop("inv_freq")
    block_pair_kernel(nc, views, onehot_rows, inv_freq, out)
    return _run(nc, [arrays], core_ids=[0]).results[0]["out"]
```

```python
import math
from contextlib import ExitStack

import numpy as np

import concourse.bass as bass
from concourse import mybir

F32 = mybir.dt.float32
F32R = mybir.dt.float32r
I32 = mybir.dt.int32
U32 = mybir.dt.uint32
ALU = mybir.AluOpType
ACT = mybir.ActivationFunctionType
AX_X = mybir.AxisListType.X

P = 128
T = 512
NT = T // P
D = 1024
KD = D // P
EPS = 1e-6
NEG = -1e30
TAKEN = -3e38
HD = 64
NH = 8
WIN = 128
BUCKETS = 32
TAPS = 31
CC = 4
FF = 2816
KF = FF // P
SKEW = 3 * P
GR = 4
TOPK = min(256, T // 4)
ROUND = float(1.5 * 2 ** 23)
TURN = [6.28125, 0.0019354820251464844, -1.7484556025237907e-07]
PI_BELOW = 3.1415925
NROT = 16 + 8
NEXP = 128
PH = 8
SEL = 16
WIDE, NARROW = 4, 4
NSUM = WIDE * SEL + (SEL - WIDE) * NARROW
HS = PH * SEL
EG = 4
NGRP = NEXP // EG
TOK4 = 4
GTOK = 64
NGT = T // GTOK
NQ = 4

NR, NW = 3, 3
RING = 2


def t5_bucket(dist):
    exact = BUCKETS // 2
    if dist < exact:
        return dist
    large = np.float32(np.log(np.float32(dist) / np.float32(exact))) / np.float32(math.log(WIN / exact))
    return min(exact + int(np.float32(large) * np.float32(BUCKETS - exact)), BUCKETS - 1)


def shape_constants():
    onehot = np.zeros((BUCKETS + 1, SKEW), np.float32)
    for m in range(SKEW):
        dist = 2 * P - 1 - m
        onehot[t5_bucket(dist) if 0 <= dist < WIN else BUCKETS, m] = 1.0
    inv = [np.power(np.float32(500000.0), -np.arange(n, dtype=np.float32) * np.float32(2.0) / np.float32(2 * n))
           for n in (16, 8)]
    return onehot, np.concatenate(inv).astype(np.float32).reshape(1, NROT)


def block_pair_kernel(nc, A, onehot_rows, inv_freq, out):
    w_in = A["w_in"]
    conv_in = NH * HD + 2 * 2 * HD

    ctx = ExitStack()
    with ctx:
        def sb(name, shape, dt=F32, scope=ctx):
            return scope.enter_context(nc.sbuf_tensor(name, shape, dt))

        sems = {}

        def s(name):
            if name not in sems:
                sems[name] = ctx.enter_context(nc.semaphore(name))
            return sems[name]

        banks = [ctx.enter_context(nc.psum_tensor(f"bank{b}", [P, 512], F32)) for b in range(8)]
        number = {}

        def bank_of(key):
            return banks[number[key] % 8]

        def wait_full(eng, key):
            n = number[key]
            eng.wait_ge(s(f"full{n % 8}"), n // 8 + 1)
            return banks[n % 8]

        def wait_read(eng, key):
            n = number[key]
            eng.wait_ge(s(f"free{n % 8}"), n // 8 + 1)

        def frees(key):
            return s(f"free{number[key] % 8}")

        units = []
        unit_at = {}

        def unit(key, k, n, parts):
            unit_at[key] = len(units)
            units.append((k, n, parts))

        def chunked(w):
            return w.rearrange("(k p) n -> p k n", p=P)

        win = chunked(w_in)
        QW = NH * HD
        for c in range(CC):
            for name, first in (("cg", conv_in + 512), ("ca", conv_in)):
                unit((name, c), KD, P, [(0, win[:, :, first + c * P:first + (c + 1) * P])])
        for kv in range(2):
            cols = win[:, :, QW + kv * HD:QW + (kv + 1) * HD]
            unit(("kk", kv), KD, P, [(0, cols), (HD, cols)])
        unit(("v", 0), KD, P, [(0, win[:, :, QW + 2 * HD:QW + 4 * HD])])
        for c in range(4):
            unit(("q", c), KD, P, [(0, win[:, :, c * P:(c + 1) * P])])
        pw = chunked(A["w_conv_pw"])
        for c in range(2):
            unit(("pw", c), CC, 2 * P, [(0, pw[:, :, c * 2 * P:(c + 1) * 2 * P])])
        wo = chunked(A["w_out"])
        for c in range(KD):
            unit(("wo", c), KD, P, [(0, wo[:, :, c * P:(c + 1) * P])])
        wg, wu, wd = chunked(A["w_gate"]), chunked(A["w_up"]), chunked(A["w_down"])
        for c in range(KF):
            unit(("wg", c), KD, P, [(0, wg[:, :, c * P:(c + 1) * P])])
            unit(("wu", c), KD, P, [(0, wu[:, :, c * P:(c + 1) * P])])
        DOWN = [(0, 8), (8, 16), (16, KF)]
        for c in range(KD):
            for j, (k0, k1) in enumerate(DOWN):
                unit(("wd", c, j), k1 - k0, P, [(0, wd[:, k0:k1, c * P:(c + 1) * P])])
        w2 = chunked(A["w_in_2"][0])
        for c in range(4):
            unit(("u2", c), KD, P, [(0, w2[:, :, c * P:(c + 1) * P])])
        NAT = [("vn", 512), ("qn", 1024), ("ci", 1536)]
        for name, first in (NAT[2], NAT[1], NAT[0]):
            for j in range(4):
                unit((name, j), 2, 512, [(0, w2[:, 2 * j:2 * j + 2, first:first + 512])])
            if name == "ci":
                unit(("kw", 0), KD, 68, [(0, w2[:, :, 2048:2116])])
        for c in range(16):
            unit(("gt", c), KD, P, [(0, w2[:, :, 2116 + c * P:2116 + (c + 1) * P])])
        wa, wb, wo2 = chunked(A["w_a_out_2"][0]), chunked(A["w_b_out_2"][0]), chunked(A["w_o_2"][0])
        for c in range(4):
            unit(("wa", c), 4, 2 * P, [(0, wa[:, :, c * 2 * P:(c + 1) * 2 * P])])
            unit(("wb", c), 4, 2 * P, [(0, wb[:, :, c * 2 * P:(c + 1) * 2 * P])])
        for c in range(KD):
            unit(("wo2", c), KD, P, [(0, wo2[:, :, c * P:(c + 1) * P])])
        wq = chunked(A["peer_wq_2"][0])
        for c in range(2 * PH):
            unit(("wq", c), KD, P, [(0, wq[:, :, c * P:(c + 1) * P])])

        def heads_of(i, per):
            first = (i // 2) * 2 * per + i % 2
            return slice(first, first + 2 * per - 1, 2)

        squares_before = [0, KD, KD + CC, 2 * KD + CC, 3 * KD + CC, 4 * KD + CC, 5 * KD + CC]
        squares_signalled = [n - m for m, n in enumerate(squares_before)]

        ident = sb("ident", [P, P])
        ones = sb("ones", [P, P])
        eps = sb("eps", [P, 1])
        vrows = sb("vrows", [P, P])
        dwrows = sb("dwrows", [P, P])
        vec = sb("vec", [P, 64])
        taps = sb("taps", [P, P])
        hT = sb("hT", [P, KD, T])
        XH = sb("XH", [P, KD, T], F32R)
        XL = sb("XL", [P, KD, T], F32R)
        sq = sb("sq", [P, RING, T])
        rt = sb("rt", [P, T])
        rstd = sb("rstd", [P, T])
        xn = sb("xn", [P, RING, T])
        stream_scope = ctx.enter_context(ExitStack())
        wraw = sb("wraw", [P, NR, 1024], F32, stream_scope)
        WH = sb("WH", [P, NW, 1024], F32R, stream_scope)
        WL = sb("WL", [P, NW, 1024], F32R, stream_scope)
        y = sb("y", [P, KD, T], F32, stream_scope)

        VROWS = [("mix_pre", A["mix_pre_g"], KD), ("mix_post", A["mix_post_g"], KD), ("ffn_pre", A["ffn_pre_g"], KD),
                 ("ffn_post", A["ffn_post_g"], KD), ("norm1", A["norm1_g_2"][0], KD), ("norm2", A["norm2_g_2"][0], KD),
                 ("dw_b", A["conv_dw_b"], CC), ("ln_g", A["conv_ln_g"], CC), ("ln_b", A["conv_ln_b"], CC)]
        vec_col, at = {}, 0
        for name, src, n in VROWS:
            vec_col[name] = at
            at += n
        NV = at

        def vcol(name, c):
            return vec[:, vec_col[name] + c:vec_col[name] + c + 1]

        x_nat = y[:, :, :].rearrange("p (t a) b -> p t (a b)", t=NT)
        with ExitStack() as sc:
            hpad = sb("hpad", [P, CC, TAPS - 1 + T], F32, sc)
            cacc = sb("cacc", [P, CC, T], F32, sc)
            sg = sb("sg", [P, 2, T], F32, sc)
            kk = sb("kk", [P, 2, T], F32, sc)
            v1 = sb("v1", [P, NT, P], F32, sc)
            q1 = sb("q1", [P, 4, T], F32, sc)
            biasT = sb("biasT", [P, NH, 2 * P], F32, sc)
            sc1 = sb("sc1", [P, 2, NH, 2 * P], F32, sc)
            pT1 = sb("pT1", [P, NH, 2, P], F32, sc)
            sinkb = sb("sinkb", [P, NH], F32, sc)
            st1 = sb("st1", [P, 2, 8, NH], F32, sc)
            relb = sb("relb", [BUCKETS + 1, NH], F32, sc)
            relbB = sb("relbB", [BUCKETS + 1, NH, P], F32, sc)
            oneh = sb("oneh", [BUCKETS + 1, SKEW], F32, sc)
            cln = sb("cln", [P, 2, T], F32, sc)
        tapped = [xn[:, 0, :], xn[:, 1, :], cln[:, 0, :], cln[:, 1, :]]
        taps_plan = [2] * 7 + [6, 6, 4]
        brow = sc1[:, :, :, :].rearrange("p a h n -> p (a h n)")[:, 0:NH * SKEW].rearrange("p (h n) -> p h n", h=NH)
        skew_dram = nc.dram_tensor("skew_rows", (P, NH, SKEW), F32).ap()
        with ExitStack() as sc:
            fH = sb("fH", [P, KF, T], F32R, sc)
            fL = sb("fL", [P, KF, T], F32R, sc)
        with ExitStack() as sc:
            ug = sb("ug", [P, GR, T], F32, sc)
            gt = sb("gt", [P, 2 * KD, T], F32, sc)
            vga = sb("vga", [P, 4, T], F32, sc)
            vv = sb("vv", [P, NT, P], F32, sc)
            qkT = sb("qkT", [P, 5, T], F32, sc)
            qiT = sb("qiT", [P, 3, T], F32, sc)
            rl = sb("rl", [P, 2, T], F32, sc)
            pT2 = sb("pT2", [P, NT, 4, P], F32, sc)
            wT = sb("wT", [P, GR, P], F32, sc)
            wukv = sb("wukv", [P, 2, 2 * P], F32, sc)
            gkv = sb("gkv", [P, 2 * P], F32, sc)
            gqk = sb("gqk", [P, 2, P], F32, sc)
            causal = sb("causal", [P, P], F32, sc)
            ck = sb("ck", [P, NT, 2 * P], F32, sc)
            widx = sb("widx", [P, NT, 4], F32, sc)
            cosin = sb("cosin", [P, 2, NT, NROT], F32, sc)
            st2 = sb("st2", [P, 96], F32, sc)
            posi = sb("posi", [P, NT], I32, sc)
            posf = sb("posf", [P, NT], F32, sc)
            invb = sb("invb", [P, NROT], F32, sc)
            m8 = sb("m8", [P, 8], F32, sc)
        pflat = pT2[:, :, :, :].rearrange("p a b c -> p (a b c)")
        gvb = pflat[:, 0:1024].rearrange("p (a n) -> p a n", a=2)
        wsr = pflat[:, 1024:1536].rearrange("p (g n) -> p g n", g=GR)
        bsb = pflat[:, 1536:2048].rearrange("p (g n) -> p g n", g=GR)
        yflat = y[:, :, :].rearrange("p a b -> p (a b)")
        qk = yflat[:, 0:NT * 5 * P].rearrange("p (t h d) -> p t h d", t=NT, h=5)
        qi = yflat[:, NT * 5 * P:NT * 5 * P + NT * 6 * HD].rearrange("p (t h d) -> p t h d", t=NT, h=6)
        isc, madd = xn[:, 0, :], xn[:, 1, :]
        cnT = sq

        def rt_angle(f):
            return rt[:, f * P:f * P + NT * NROT]

        css, kss, vsum, vss = st2[:, 0:4], st2[:, 4:24], st2[:, 24:28], st2[:, 28:32]
        crs, krs, vrs, nmean = st2[:, 32:36], st2[:, 36:56], st2[:, 56:60], st2[:, 60:64]
        amax, ansum, arec = st2[:, 64:68], st2[:, 68:72], st2[:, 72:76]
        vmean = st2[:, 76:80]
        with ExitStack() as sc:
            skn = sb("skn", [P, 2 * PH, P], F32, sc)
            skT = sb("skT", [P, 2 * PH, P], F32, sc)
            qq = sb("qq", [P, 2, T], F32, sc)
            subs = sb("subs", [P, 4, NT, P], F32, sc)
            wk = sb("wk", [P, NT, 2 * P], F32, sc)
            cand = sb("cand", [P, NT, NSUM], F32, sc)
            stop = sb("stop", [P, NT, 2 * PH, SEL], F32, sc)
            itop = sb("itop", [P, NT, 2 * PH, SEL], U32, sc)
            itf = sb("itf", [P, PH, 2 * NT, SEL], F32, sc)
            best = sb("best", [P, NT, PH, SEL], F32, sc)
            bpos = sb("bpos", [P, NT, PH, SEL], U32, sc)
            bits = sb("bits", [P, 2, 5, NT * SEL], U32, sc)
            bitf = sb("bitf", [P, 2, 5, NT * SEL], F32, sc)
            bdif = sb("bdif", [P, 2, 2, NT * SEL], F32, sc)
            bhf = sb("bhf", [P, PH, 2, NT, SEL], F32, sc)
            hot = sb("hot", [P, 2, 2 * NT, SEL, SEL], F32, sc)
            sel = sb("sel", [P, 3, NT, HS], F32, sc)
            iota16 = sb("iota16", [P, SEL], F32, sc)
            bsum = sb("bsum", [P, NT * PH], F32, sc)
        ijcol, gcol = sq, rt
        stream_scope.close()
        gd = nc.dram_tensor("gate_matrices", (NGT, P, NEXP, GTOK), F32).ap()
        with ExitStack() as sc:
            Gs = sb("Gs", [P, 2, NEXP, GTOK], F32, sc)
            hots = sb("hots", [P, NQ, 2, TOK4, P], F32, sc)
            iota128 = sb("iota128", [P, P], F32, sc)
            uraw = sb("uraw", [P, EG, D], F32, sc)
            vraw = sb("vraw", [P, EG, D], F32, sc)
            UH = sb("UH", [P, 2, KD, P], F32R, sc)
            UL = sb("UL", [P, 2, KD, P], F32R, sc)
            ac = sb("ac", [P, 2, T], F32, sc)
            ga = sb("ga", [P, 2, T], F32, sc)
        with ExitStack() as sc:
            VH = sb("VH", [P, EG, D], F32R, sc)
            VL = sb("VL", [P, EG, D], F32R, sc)
            gr = sb("gr", [P, EG, T], F32, sc)
            GH = sb("GH", [P, EG, T], F32R, sc)
            GL = sb("GL", [P, EG, T], F32R, sc)
        o_sb = uraw[:, :, :].rearrange("p a b -> p (a b)")
        LAST = NGRP - 1
        block = ctx.enter_context(nc.Block())

        @block.tensor
        def _(pe):
            taken = [0]

            def take(*key):
                n = taken[0]
                taken[0] += 1
                number[key] = n
                if n >= 8:
                    pe.wait_ge(s(f"free{n % 8}"), n // 8)
                return banks[n % 8]

            def full(last, *key):
                last.then_inc(s(f"full{number[key] % 8}"), 1)

            def split(out, wh, wl, xh, xl, first, last, begins=False):
                mm = pe.matmul(out, wh, xh, start=first, stop=False)
                if begins:
                    mm.then_inc(s("w_begun"), 1)
                pe.matmul(out, wh, xl, start=False, stop=False)
                return pe.matmul(out, wl, xh, start=False, stop=last)

            def unit_views(key):
                u = unit_at[key]
                k, n, _ = units[u]
                pe.wait_ge(s("w_lo"), u + 1)
                return [w[:, u % NW, 0:k * n].rearrange("p (k n) -> p k n", k=k) for w in (WH, WL)]

            def project(key, out, k0=0, col=0, first=True, last=True, x0=0, ready=None):
                wh, wl = unit_views(key)
                n = units[unit_at[key]][0]
                for k in range(n):
                    if ready:
                        pe.wait_ge(s(ready[0]), ready[1] + k + 1)
                    mm = split(out, wh[:, k, col:col + P], wl[:, k, col:col + P], XH[:, x0 + k, :], XL[:, x0 + k, :],
                               first and k == 0, last and k == n - 1, begins=k == 0 and col == 0)
                return mm

            def tile(unit_key, key, **kw):
                out = take(*key)
                full(project(unit_key, out[:, :], **kw), *key)

            def square_sum(m, chunks=KD):
                take("ss", m)
                for k in range(chunks):
                    add_square(m, k, chunks)

            def add_square(m, k, chunks=KD):
                pe.wait_ge(s("squares"), squares_before[m] + k + 1)
                mm = pe.matmul(bank_of(("ss", m))[:, :], ones[:, :], sq[:, k % RING, :], start=k == 0,
                               stop=k == chunks - 1)
                if k < chunks - 1:
                    mm.then_inc(s("squares_used"), 1)
                else:
                    full(mm, "ss", m)

            def prepare():
                pe.wait_ge(s("ident_made"), 2)
                pe.wait_ge(s("vrows_landed"), 16 * len(VROWS))
                pe.wait_ge(s("ones_made"), 2)
                out = take("vec", 0)
                full(pe.transpose(out[:, 0:NV], vrows[0:NV, :], ident[0:NV, 0:NV]), "vec", 0)
                pe.wait_ge(s("taps_landed"), 16)
                out = take("vec", 1)
                n = TAPS * CC
                full(pe.transpose(out[:, 0:n], dwrows[0:n, :], ident[0:n, 0:n]), "vec", 1)
                for t in range(NT):
                    pe.wait_ge(s(f"x_landed{t}"), 16)
                for k in range(KD):
                    out = take("xT", k)
                    for t in range(NT):
                        mm = pe.transpose(out[:, t * P:(t + 1) * P], x_nat[:, t, k * P:(k + 1) * P], ident[:, :])
                    full(mm, "xT", k)
                square_sum(0)
                pe.wait_ge(s("relb_spread"), 1)
                for h in range(NH):
                    out = take("brow", h)
                    full(pe.matmul(out[:, 0:SKEW], relbB[:, h, :], oneh[:, :], start=True, stop=True), "brow", h)

            def first_projections():
                for c in range(CC):
                    tile(("cg", c), ("cg", c), ready=("x_lo", 0) if c == 0 else None)
                    tile(("ca", c), ("ca", c))
                for kv in range(2):
                    tile(("kk", kv), ("kk", kv))
                out = take("v", 0)
                wh, wl = unit_views(("v", 0))
                for t in range(NT):
                    for k in range(KD):
                        mm = split(out[:, t * P:(t + 1) * P], XH[:, k, t * P:(t + 1) * P], XL[:, k, t * P:(t + 1) * P],
                                   wh[:, k, :], wl[:, k, :], k == 0, k == KD - 1, begins=t == k == 0)
                full(mm, "v", 0)
                for c in range(4):
                    tile(("q", c), ("q", c))

            def scores(b):
                if b == 0:
                    for key in (("kk", 0), ("kk", 1), ("v", 0)) + tuple(("q", c) for c in range(4)):
                        wait_read(pe, key)
                w = P if b == 0 else 2 * P
                k0 = max(b - 1, 0) * P
                per = 512 // w
                for i in range(NH // per):
                    out = take("sc", b, i)
                    for j in range(per):
                        h = heads_of(i, per).start + 2 * j
                        half = slice((h % 2) * HD, (h % 2) * HD + HD)
                        mm = pe.matmul(out[:, j * w:(j + 1) * w], q1[half, h // 2, b * P:(b + 1) * P],
                                       kk[half, h // 4, k0:k0 + w], start=True, stop=True)
                    full(mm, "sc", b, i)

            def weighted_values(b):
                kts = [1] if b == 0 else [0, 1]
                pe.wait_ge(s("probs"), b + 1)
                for i in range(NH // 2):
                    out = take("pT", b, i)
                    for j in range(2):
                        for kt in kts:
                            w = (kt if b else 0) * P
                            mm = pe.transpose(out[:, (2 * j + kt) * P:(2 * j + kt + 1) * P],
                                              sc1[:, b % 2, 2 * i + j, w:w + P], ident[:, :])
                    full(mm, "pT", b, i)
                out = take("o", b)
                for h in range(NH):
                    if h % 2 == 0:
                        wait_read(pe, ("pT", b, h // 2))
                    half = slice((h % 2) * HD, (h % 2) * HD + HD)
                    kv = slice((h // 4) * HD, (h // 4) * HD + HD)
                    for kt in kts:
                        mm = pe.matmul(out[half, (h // 2) * P:(h // 2 + 1) * P], v1[:, b - 1 + kt, kv],
                                       pT1[:, h, kt, :], start=kt == kts[0], stop=kt == 1)
                full(mm, "o", b)

            def attention():
                scores(0)
                scores(1)
                for b in range(NT):
                    if b + 2 < NT:
                        scores(b + 2)
                    weighted_values(b)

            def conv_tail():
                out = take("cmean", 0)
                for c in range(CC):
                    if c < CC - 1:
                        pe.wait_ge(s("conv_done"), c + 1)
                    else:
                        pe.wait_ge(s("taps_added"), TAPS - 1)
                    mm = pe.matmul(out[:, :], ones[:, :], cacc[:, c, :], start=c == 0, stop=c == CC - 1)
                full(mm, "cmean", 0)
                square_sum(1, CC)
                for c in range(2):
                    for j in range(2):
                        out = take("pw", 2 * c + j)
                        mm = project(("pw", c), out[:, :], col=j * P, x0=4,
                                     ready=("conv_lo", 0) if c == j == 0 else None)
                        full(mm, "pw", 2 * c + j)

            def mix_out():
                for key in [("o", b) for b in range(NT)] + [("pw", c) for c in range(CC)]:
                    wait_read(pe, key)
                for c in range(KD):
                    tile(("wo", c), ("y", 0, c))
                    if c == 0:
                        take("ss", 2)
                    else:
                        add_square(2, c - 1)
                add_square(2, KD - 1)
                square_sum(3)

            def feed_forward():
                for c in range(KF):
                    tile(("wg", c), ("fg", c), ready=("x_lo", KD) if c == 0 else None)
                    tile(("wu", c), ("fu", c))
                for c in range(KD):
                    out = take("y", 1, c)
                    for j, (k0, k1) in enumerate(DOWN):
                        wh, wl = unit_views(("wd", c, j))
                        for k in range(k0, k1):
                            if c == 0:
                                pe.wait_ge(s("f_lo"), k + 1)
                            mm = split(out[:, :], wh[:, k - k0, :], wl[:, k - k0, :], fH[:, k, :], fL[:, k, :], k == 0,
                                       k == KF - 1, begins=k == k0)
                    full(mm, "y", 1, c)
                    if c == 0:
                        take("ss", 4)
                    else:
                        add_square(4, c - 1)
                add_square(4, KD - 1)
                square_sum(5)

            def store_out(src, signal):
                for t in range(NT):
                    for half in range(2):
                        out = take("out", t, half)
                        if t == half == 0:
                            signal(pe)
                        for k in range(4):
                            mm = pe.transpose(out[:, k * P:(k + 1) * P], src[:, half * 4 + k, t * P:(t + 1) * P],
                                              ident[:, :])
                        full(mm, "out", t, half)

            def natural(name, key0):
                outs = [take(name, t) for t in range(NT)]
                for j in range(4):
                    wh, wl = unit_views((name, j))
                    for t in range(NT):
                        tok = slice(t * P, (t + 1) * P)
                        for i in range(2):
                            k = 2 * j + i
                            mm = split(outs[t][:, :], XH[:, k, tok], XL[:, k, tok], wh[:, i, :], wl[:, i, :], k == 0,
                                       k == KD - 1, begins=t == i == 0)
                        if j == 3:
                            full(mm, name, t)

            def second_projections():
                for c in range(4):
                    tile(("u2", c), ("u2", c), ready=("x_lo", 2 * KD) if c == 0 else None)
                natural("ci", 1536)
                out = take("kw", 0)
                wh, wl = unit_views(("kw", 0))
                for t in range(NT):
                    for k in range(KD):
                        mm = split(out[:, t * 68:(t + 1) * 68], XH[:, k, t * P:(t + 1) * P], XL[:, k, t * P:(t + 1) * P],
                                   wh[:, k, :], wl[:, k, :], k == 0, k == KD - 1, begins=t == k == 0)
                full(mm, "kw", 0)
                natural("qn", 1024)
                pe.wait_ge(s("cn_made"), NT)
                for j in range(2):
                    out = take("cT", j)
                    for t in range(NT):
                        mm = pe.transpose(out[:, t * P:(t + 1) * P], ck[:, t, j * P:(j + 1) * P], ident[:, :])
                    full(mm, "cT", j)
                natural("vn", 512)
                pe.wait_ge(s("wukv_landed"), 32)
                for i in range(2):
                    out = take("kv", i)
                    for t in (2 * i, 2 * i + 1):
                        for j in range(2):
                            if i == 0:
                                wait_read(pe, ("cT", j))
                            mm = pe.matmul(out[:, (t % 2) * 256:(t % 2) * 256 + 256], cnT[:, j, t * P:(t + 1) * P],
                                           wukv[:, j, :], start=j == 0, stop=j == 1)
                    full(mm, "kv", i)

            def second_transposes():
                pe.wait_ge(s("spatial_masked"), 1)
                out = take("wT", 0)
                for g in range(GR):
                    mm = pe.transpose(out[:, g * P:(g + 1) * P], wsr[:, g, :], ident[:, :])
                full(mm, "wT", 0)
                wait_read(pe, ("wT", 0))
                for t in range(NT):
                    pe.wait_ge(s("v_normed"), t + 1)
                    out = take("z", t)
                    for g in range(GR):
                        mm = pe.matmul(out[:, g * P:(g + 1) * P], vga[:, t, g * P:(g + 1) * P], wT[:, g, :],
                                       start=True, stop=True)
                    full(mm, "z", t)
                pe.wait_ge(s("rotated"), 2)
                for h in range(3):
                    out = take("iT", h)
                    for t in range(NT):
                        mm = pe.transpose(out[:, t * P:(t + 1) * P],
                                          qi[:, t, 2 * h:2 * h + 2, :].rearrange("p h d -> p (h d)"), ident[:, :])
                    full(mm, "iT", h)
                for h in range(5):
                    out = take("hT", h)
                    for t in range(NT):
                        mm = pe.transpose(out[:, t * P:(t + 1) * P], qk[:, t, h, :], ident[:, :])
                    full(mm, "hT", h)

            def sparse_attention():
                for b in range(NT):
                    n = (b + 1) * P
                    tok = slice(b * P, (b + 1) * P)
                    if b == 0:
                        for h in range(3):
                            wait_read(pe, ("iT", h))
                        for h in range(5):
                            wait_read(pe, ("hT", h))
                    for h in range(4):
                        out = take("ix", b, h)
                        half = slice((h % 2) * HD, (h % 2) * HD + HD)
                        full(pe.matmul(out[:, 0:n], qiT[half, h // 2, tok], qiT[half, 2, 0:n], start=True, stop=True),
                             "ix", b, h)
                    for h in range(4):
                        out = take("at", b, h)
                        full(pe.matmul(out[:, 0:n], qkT[:, h, tok], qkT[:, 4, 0:n], start=True, stop=True), "at", b, h)
                    for c in range(4):
                        tile(("gt", 4 * b + c), ("gt", 4 * b + c))
                    pe.wait_ge(s("probs2"), b + 1)
                    for kt in range(b + 1):
                        out = take("pT2", b, kt)
                        for h in range(4):
                            mm = pe.transpose(out[:, h * P:(h + 1) * P], vga[:, h, kt * P:(kt + 1) * P], ident[:, :])
                        full(mm, "pT2", b, kt)
                    out = take("yb", b)
                    for kt in range(b + 1):
                        wait_read(pe, ("pT2", b, kt))
                        mm = pe.matmul(out[:, :], vv[:, kt, :], pT2[:, kt, :, :].rearrange("p h q -> p (h q)"),
                                       start=kt == 0, stop=kt == b)
                    full(mm, "yb", b)

            def merge_and_out():
                for u in range(KD // 2):
                    for j, name in enumerate(("wa", "wb")):
                        for c in (2 * u, 2 * u + 1):
                            out = take(name, c)
                            full(project((name, u), out[:, :], col=(c % 2) * P, x0=4 * j,
                                         ready=("branch_lo", 4 * j) if c == 0 else None), name, c)
                for c in range(KD):
                    tile(("wo2", c), ("o2", c), ready=("merged_lo", 0) if c == 0 else None)
                square_sum(6)

            def choose_experts():
                pe.wait_ge(s("subkeys_landed"), 16)
                for q in range(4):
                    out = take("sk", q)
                    for r in range(4):
                        mm = pe.transpose(out[:, r * P:(r + 1) * P], skn[:, 4 * q + r, :], ident[:, :])
                    full(mm, "sk", q)

                def sub(hp):
                    wait_read(pe, ("q2", hp))
                    wait_read(pe, ("sk", hp // 4))
                    out = take("sub", hp)
                    for t in range(NT):
                        mm = pe.matmul(out[:, t * P:(t + 1) * P], qq[:, hp % 2, t * P:(t + 1) * P], skT[:, hp, :],
                                       start=True, stop=True)
                    full(mm, "sub", hp)

                for hp in range(2 * PH):
                    tile(("wq", hp), ("q2", hp), ready=("x_lo", 3 * KD) if hp == 0 else None)
                    if hp:
                        sub(hp - 1)
                sub(2 * PH - 1)
                pe.wait_ge(s("summed"), PH)
                for t in range(NT):
                    out = take("sel", t)
                    for j in range(3):
                        mm = pe.transpose(out[:, j * P:(j + 1) * P], sel[:, j, t, :], ident[:, :])
                    full(mm, "sel", t)

            def gate_matrices():
                for n in range(taken[0] - 8, taken[0]):
                    pe.wait_ge(s(f"free{n % 8}"), n // 8 + 1)
                pe.sem_inc(s("g_full"), NQ)
                for tt in range(NGT):
                    with pe.Fori(0, GTOK // (NQ * TOK4)) as n:
                        for q in range(NQ):
                            four = n * NQ + (tt * GTOK // TOK4 + q)
                            pe.wait_ge(s("hots_weighed"), four + 1)
                            pe.wait_ge(s("g_copied"), four + 1)
                            for r in range(TOK4):
                                mm = pe.matmul(banks[q][:, r * P:(r + 1) * P], hots[:, q, 1, r, :], hots[:, q, 0, r, :],
                                               start=True, stop=True)
                            mm.then_inc(s("g_full"), 1)

            def experts():
                def turn(x, e):
                    pe.wait_ge(s(f"u_landed{e}"), (x - e) * 4 + 16)
                    for half in range(2):
                        pe.wait_ge(s("ut_lo"), x * 2 + half + 1)
                        for k in range(4):
                            mm = pe.transpose(banks[half][:, k * P:(k + 1) * P],
                                              uraw[:, e, (half * 4 + k) * P:(half * 4 + k + 1) * P], ident[:, :])
                        mm.then_inc(s("ut_full"), 1)

                def up(x, b):
                    pe.wait_ge(s("ut_lo"), x * 2 + 4)
                    pe.wait_ge(s("gelu"), x + 1)
                    for k in range(KD):
                        mm = split(banks[2 + b][:, :], UH[:, b, k, :], UL[:, b, k, :], XH[:, k, :], XL[:, k, :],
                                   k == 0, k == KD - 1)
                    mm.then_inc(s("up_full"), 1)

                def down(g):
                    pe.wait_ge(s("ga_lo"), g * EG + EG + 2)
                    pe.wait_ge(s("v_lo"), g * EG + EG)
                    for c in range(KD):
                        pe.wait_ge(s("added"), g * KD + c + 1)
                        for e in range(EG):
                            cols = slice(c * P, (c + 1) * P)
                            mm = split(banks[4 + c % 2][:, :], VH[:, e, cols], VL[:, e, cols], GH[:, e, :], GL[:, e, :],
                                       e == 0, e == EG - 1)
                        mm.then_inc(s("down_full"), 1)

                pe.wait_ge(s("g_copied"), T // TOK4 + NQ)
                pe.sem_inc(s("up_full"), 2)
                pe.sem_inc(s("down_full"), 1)
                turn(0, 0)
                turn(1, 1)
                up(0, 0)
                with pe.Fori(0, LAST) as g:
                    for e in range(1, EG + 1):
                        x = g * EG + e
                        turn(x + 1, (e + 1) % EG)
                        up(x, e % 2)
                    down(g)
                for x in range(LAST * EG + 1, NEXP):
                    if x + 1 < NEXP:
                        turn(x + 1, (x + 1) % EG)
                    up(x, x % 2)
                down(LAST)

            prepare()
            first_projections()
            attention()
            conv_tail()
            mix_out()
            feed_forward()
            second_projections()
            second_transposes()
            sparse_attention()
            merge_and_out()
            choose_experts()
            gate_matrices()
            experts()
            store_out(hT, lambda eng: eng.wait_ge(s("added"), NGRP * KD + 2))

        def store(eng):
            for t in range(NT):
                for half in range(2):
                    wait_read(eng, ("out", t, half))
                eng.dma_start(out[0, t * P:(t + 1) * P, :], o_sb[:, t * D:(t + 1) * D]).then_inc(
                    s("stored"), 16)
            eng.wait_ge(s("stored"), 16 * NT)

        @block.sync
        def _(sp):
            x = A["x"][0]
            for t in range(NT):
                sp.dma_start(x_nat[:, t, :], x[t * P:(t + 1) * P, :]).then_inc(s(f"x_landed{t}"), 16)
                if t == 0:
                    at = 0
                    for name, src, n in VROWS:
                        sp.dma_start(vrows[at:at + n, :], src.rearrange("(c p) -> c p", p=P)).then_inc(s("vrows_landed"), 16)
                        at += n
                    sp.dma_start(dwrows[0:TAPS * CC, :], A["conv_dw"].rearrange("w (c p) -> (w c) p", p=P)).then_inc(
                        s("taps_landed"), 16)
                    sp.dma_start(relb[0:BUCKETS, :], A["rel_bias"]).then_inc(s("relb_landed"), 16)
                    sp.dma_start(oneh[:, :], onehot_rows).then_inc(s("relb_landed"), 16)
                    sp.dma_start(sinkb[:, :], A["attn_sinks"].rearrange("(a h) -> a h", a=1).partition_broadcast(P)).then_inc(
                        s("sinks_landed"), 16)

            def stream(u):
                k, n, parts = units[u]
                if u >= NR:
                    sp.wait_ge(s("w_lo"), u - NR + 1)
                for col, src in parts:
                    dst = wraw[:, u % NR, 0:k * n].rearrange("p (k n) -> p k n", k=k)[:, :, col:col + src.shape[2]]
                    sp.dma_start(dst, src).then_inc(s(f"w_landed{u % NR}"), 16)

            for u in range(6):
                stream(u)
            for h in range(NH):
                wait_read(sp, ("brow", h))
            sp.dma_start(skew_dram, brow[:, :, :]).then_inc(s("skew_out"), 16)
            sp.wait_ge(s("skew_out"), 16)
            back = bass.AP(skew_dram.tensor, P - 1, [[NH * SKEW - 1, P], [SKEW, NH], [1, 2 * P]])
            sp.dma_start(biasT[:, :, :], back).then_inc(s("bias_landed"), 16)
            def second_inputs():
                wait_full(sp, ("y", 1, KD - 1))
                sp.dma_start(posi[:, :], A["positions_2"].rearrange("a (t p) -> p (a t)", p=P),
                             allow_slow_non_contiguous=True).then_inc(s("pos_landed"), 16)
                sp.dma_start(invb[:, :], inv_freq.partition_broadcast(P)).then_inc(s("pos_landed"), 16)
                for j, w in enumerate(("w_uk_2", "w_uv_2")):
                    sp.dma_start(wukv[:, :, j * P:(j + 1) * P], chunked(A[w][0])).then_inc(s("wukv_landed"), 16)
                sp.dma_start(gkv[:, :], A["kv_norm_g_2"].partition_broadcast(P)).then_inc(s("gains_landed"), 16)
                sp.dma_start(gqk[:, 0, :], A["q_norm_g_2"].partition_broadcast(P)).then_inc(s("gains_landed"), 16)
                sp.dma_start(gqk[:, 1, :], A["k_norm_g_2"].partition_broadcast(P)).then_inc(s("gains_landed"), 16)
                sp.dma_start(gvb[:, 0, :], A["v_norm_g_2"].partition_broadcast(P)).then_inc(s("gains_landed"), 16)
                sp.dma_start(gvb[:, 1, :], A["v_norm_b_2"].partition_broadcast(P)).then_inc(s("gains_landed"), 16)
                sp.dma_start(bsb[:, :, :], A["spatial_b_2"].partition_broadcast(P)).then_inc(s("gains_landed"), 16)
                sp.dma_start(wsr[:, :, :], A["spatial_w_2"][0].rearrange("g t s -> t g s")).then_inc(s("wsr_landed"), 16)

            for u in range(6, len(units)):
                if u == unit_at[("u2", 0)] + 2:
                    second_inputs()
                if u == unit_at[("wq", 0)] + 2:
                    for c in range(KD):
                        wait_read(sp, ("wa", c))
                        wait_read(sp, ("wb", c))
                    sp.wait_ge(s("merged"), KD)
                    sp.dma_start(skn[:, :, :], A["peer_subkeys_2"][0].rearrange("h a n d -> n (h a) d")).then_inc(
                        s("subkeys_landed"), 16)
                stream(u)

            def gates_out():
                for tt in range(NGT):
                    sp.wait_ge(s("g_copied"), (tt + 1) * GTOK // TOK4 + NQ)
                    sp.dma_start(gd[tt], Gs[:, tt % 2, :, :]).then_inc(s(f"g_out{tt}"), 16)
                    if tt == NGT - 2:
                        for e in range(EG):
                            load_u(e, e, True)
                            load_v(e, e, True)

            u_rows = A["peer_u_2"][0].rearrange("(i j) d -> i j d", j=P)
            v_rows = A["peer_v_2"][0].rearrange("(i j) d -> i j d", j=P)
            gates = gd.rearrange("g j i t -> i j g t")

            def at_row(view, x):
                return view[x] if type(x) is int else view[bass.ds(x, 1)].squeeze(0)

            def load_u(x, e, first):
                if not first:
                    sp.wait_ge(s("ut_full"), x * 2 - 2 * EG + 2)
                sp.dma_start(uraw[:, e, :], at_row(u_rows, x)).then_inc(s(f"u_landed{e}"), 16)

            def load_v(x, e, first):
                if not first:
                    sp.wait_ge(s("v_lo"), x - EG + 1)
                sp.dma_start(vraw[:, e, :], at_row(v_rows, x)).then_inc(s(f"v_landed{e}"), 16)

            def load_gates(x, e, first):
                if not first:
                    sp.wait_ge(s("ga_f"), x - EG + 3)
                sp.dma_start(gr[:, e, :].rearrange("p (g t) -> p g t", g=NGT), at_row(gates, x)).then_inc(
                    s(f"g_landed{e}"), 16)

            def load_experts():
                for tt in range(NGT):
                    sp.wait_ge(s(f"g_out{tt}"), 16)
                for e in range(EG):
                    load_gates(e, e, True)
                with sp.Fori(1, NGRP) as g:
                    for e in range(EG):
                        x = g * EG + e
                        load_u(x, e, False)
                        load_gates(x, e, False)
                        load_v(x, e, False)

            gates_out()
            load_experts()
            store(sp)

        @block.gpsimd
        def _(pool):
            pool.memset(ones[:, :], 1.0).then_inc(s("ones_made"), 1)
            pool.memset(eps[:, :], EPS).then_inc(s("ones_made"), 1)
            pool.memset(ident[:, :], 0.0).then_inc(s("ident_made"), 1)
            pool.wait_ge(s("ident_made"), 1)
            pool.affine_select(out=ident[:, :], in_=ident[:, :], compare_op=ALU.not_equal, fill=1.0, base=0,
                               pattern=[[-1, P]], channel_multiplier=1).then_inc(s("ident_made"), 1)

            def pick(h):
                pool.wait_ge(s("rank_hots"), h + 1)
                at = hot[:, h % 2, :, :, :]
                pool.tensor_tensor(at, at, itf[:, h, :, :].unsqueeze(2).to_broadcast([P, 2 * NT, SEL, SEL]),
                                   ALU.mult).then_inc(s("picked"), 1)

            for u, (k, n, _) in enumerate(units):
                if u == unit_at[("ci", 0)]:
                    pool.wait_ge(s("wsr_landed"), 16)
                    pool.affine_select(out=wsr[:, :, :], in_=wsr[:, :, :], compare_op=ALU.is_ge, fill=0.0, base=0,
                                       pattern=[[0, GR], [-1, P]], channel_multiplier=1).then_inc(s("spatial_masked"), 1)
                    pool.memset(causal[:, :], 0.0).then_inc(s("causal_made"), 1)
                    pool.wait_ge(s("causal_made"), 1)
                    pool.affine_select(out=causal[:, :], in_=causal[:, :], compare_op=ALU.is_ge, fill=NEG, base=0,
                                       pattern=[[-1, P]], channel_multiplier=1).then_inc(s("causal_made"), 1)
                if u in (unit_at[("wq", 2 * h + 8)] for h in range(PH - 4)):
                    pick((u - unit_at[("wq", 8)]) // 2)
                if unit_at[("kk", 0)] + 2 <= u <= unit_at[("pw", 0)] + 1:
                    stage = u - unit_at[("kk", 0)] - 2
                    w0 = 1 + sum(taps_plan[:stage])
                    w1 = w0 + taps_plan[stage] if u <= unit_at[("pw", 0)] else TAPS
                    for w in range(w0, w1):
                        pool.wait_ge(s("taps_made"), w)
                        if w == 1:
                            pool.wait_ge(s("taps_begun"), 1)
                        else:
                            pool.wait_ge(s("taps_added"), w - 1)
                        pool.tensor_tensor(cacc[:, CC - 1, :], cacc[:, CC - 1, :], tapped[w % len(tapped)],
                                           ALU.add).then_inc(s("taps_added"), 1)
                pool.wait_ge(s("w_hi"), u + 1)
                if u >= NW:
                    pool.wait_ge(s("w_begun"), u - NW + 2)
                m = k * n
                if u == unit_at[("wq", 0)] + 2:
                    for c in range(KD):
                        wait_read(pool, ("wb", c))
                    pool.wait_ge(s("merged"), KD)
                    pool.iota(iota16[:, :], pattern=[[1, SEL]], base=0, channel_multiplier=0,
                              allow_small_or_imprecise_dtypes=True).then_inc(s("iota_made"), 1)
                pool.tensor_tensor(WL[:, u % NW, 0:m], wraw[:, u % NR, 0:m], WH[:, u % NW, 0:m].bitcast(F32),
                                   ALU.subtract).then_inc(s("w_lo"), 1)

            for h in range(PH - 4, PH):
                pick(h)
            for t in range(NT):
                wait_full(pool, ("sel", t))
            pool.iota(iota128[:, :], pattern=[[1, P]], base=0, channel_multiplier=0,
                      allow_small_or_imprecise_dtypes=True).then_inc(s("iota_made"), 1)
            for t in range(NT):
                wait_read(pool, ("sel", t))
            for tt in range(NGT):
                with pool.Fori(0, GTOK // (NQ * TOK4)) as n:
                    for q in range(NQ):
                        four = n * NQ + (tt * GTOK // TOK4 + q)
                        pool.wait_ge(s("hots_made"), four + 1)
                        gate = gcol[:, bass.ds(n * (NQ * TOK4) + (tt * GTOK + q * TOK4), TOK4)]
                        pool.tensor_tensor(hots[:, q, 0, :, :], hots[:, q, 0, :, :],
                                           gate.unsqueeze(2).to_broadcast([P, TOK4, P]), ALU.mult).then_inc(
                                               s("hots_weighed"), 1)
            with pool.Fori(0, NGRP) as g:
                for e in range(EG):
                    pool.wait_ge(s("v_hi"), g * EG + e + 1)
                    pool.tensor_tensor(VL[:, e, :], vraw[:, e, :], VH[:, e, :].bitcast(F32), ALU.subtract).then_inc(
                        s("v_lo"), 1)

        @block.scalar
        def _(act):
            cast = [0]
            arrived = [0] * NR

            def cast_to(key_or_u):
                u1 = key_or_u if type(key_or_u) is int else unit_at[key_or_u] + 1
                while cast[0] <= min(u1, len(units) - 1):
                    u = cast[0]
                    k, n, parts = units[u]
                    arrived[u % NR] += 16 * len(parts)
                    act.wait_ge(s(f"w_landed{u % NR}"), arrived[u % NR])
                    if u >= NW:
                        act.wait_ge(s("w_begun"), u - NW + 2)
                    act.activation(WH[:, u % NW, 0:k * n], wraw[:, u % NR, 0:k * n], ACT.Copy).then_inc(s("w_hi"), 1)
                    cast[0] += 1

            def root_mean(m, n=D):
                ss = wait_full(act, ("ss", m))
                act.activation(rt[:, :], ss[:, :], ACT.Sqrt, bias=eps[:, 0:1], scale=1.0 / n).then_inc(frees(("ss", m)), 1)

            def square(m, k, src, signal=None):
                if k >= RING:
                    act.wait_ge(s("squares_used"), squares_signalled[m] + k - RING + 1)
                act.activation(sq[:, k % RING, :], src, ACT.Square).then_inc(s("squares"), 1)

            def high_of_norm(n):
                for k in range(KD):
                    act.wait_ge(s("xn"), n * KD + k + 1)
                    act.activation(XH[:, k, :], xn[:, k % RING, :], ACT.Copy).then_inc(s("x_hi"), 1)

            def prepare():
                act.wait_ge(s("ones_made"), 2)
                cast_to(1)
                for k in range(KD):
                    src = wait_full(act, ("xT", k))
                    act.activation(hT[:, k, :], src[:, :], ACT.Copy).then_inc(frees(("xT", k)), 1)
                    wait_read(act, ("xT", k))
                    square(0, k, hT[:, k, :])
                root_mean(0)
                high_of_norm(0)
                for h in range(NH):
                    src = wait_full(act, ("brow", h))
                    act.activation(brow[:, h, :], src[:, 0:SKEW], ACT.Copy).then_inc(frees(("brow", h)), 1)

            def first_projections():
                for c in range(CC):
                    cast_to(("cg", c))
                    src = wait_full(act, ("cg", c))
                    if c >= 2:
                        wait_read(act, ("ca", c - 2))
                    act.activation(sg[:, c % 2, :], src[:, :], ACT.Sigmoid).then_inc(frees(("cg", c)), 1)
                    cast_to(("ca", c))
                for key, dst in [(("kk", 0), kk[:, 0, :]), (("kk", 1), kk[:, 1, :]),
                                 (("v", 0), v1[:, :, :].rearrange("p t n -> p (t n)"))] + [
                                     (("q", c), q1[:, c, :]) for c in range(4)]:
                    cast_to(key)
                    src = wait_full(act, key)
                    act.activation(dst, src[:, :], ACT.Copy).then_inc(frees(key), 1)
                    last_chunk_taps()

            tapped_by_act, stages = [0], iter(taps_plan)

            def last_chunk_taps():
                c, w = CC - 1, tapped_by_act[0]
                if w == 0:
                    wait_read(act, ("ca", c))
                    act.wait_ge(s("x_lo"), KD)
                    act.activation(cacc[:, c, :], hpad[:, c, 0:T], ACT.Identity, bias=vcol("dw_b", c),
                                   scale=taps[:, c:c + 1]).then_inc(s("taps_begun"), 1)
                    w = 1
                for w in range(w, w + next(stages, 0)):
                    if w > len(tapped):
                        act.wait_ge(s("taps_added"), w - len(tapped))
                    act.activation(tapped[w % len(tapped)], hpad[:, c, w:w + T], ACT.Copy,
                                   scale=taps[:, w * CC + c:w * CC + c + 1]).then_inc(s("taps_made"), 1)
                    tapped_by_act[0] = w + 1

            def attention():
                for b in range(NT):
                    w = P if b == 0 else 2 * P
                    st = st1[:, b % 2]
                    act.wait_ge(s("sink_gap"), b + 1)
                    for h in range(NH):
                        act.activation(sc1[:, b % 2, h, 0:w], sc1[:, b % 2, h, 0:w], ACT.Exp, bias=st[:, 1, h:h + 1],
                                       accum_out=st[:, 2, h:h + 1])
                    act.activation(st[:, 4, :], st[:, 3, :], ACT.Exp).then_inc(s("exps"), 1)
                    last_chunk_taps()
                    for i in range(NH // 2):
                        src = wait_full(act, ("pT", b, i))
                        kt0 = 1 if b == 0 else 0
                        if b and i == 0:
                            wait_full(act, ("o", b - 1))
                        act.activation(pT1[:, 2 * i:2 * i + 2, kt0:2, :],
                                       src[:, :].rearrange("p (h t q) -> p h t q", h=2, t=2)[:, :, kt0:2, :],
                                       ACT.Copy).then_inc(frees(("pT", b, i)), 1)
                    src = wait_full(act, ("o", b))
                    act.activation(XH[:, 0:4, b * P:(b + 1) * P], src[:, :].rearrange("p (c q) -> p c q", c=4),
                                   ACT.Copy).then_inc(s("att_hi"), 1)

            def conv_tail():
                for c in range(CC):
                    act.wait_ge(s("centred"), c + 1)
                    square(1, c, cacc[:, c, :])
                root_mean(1, CC * P)
                for c in range(CC):
                    act.wait_ge(s("ln_scaled"), c + 1)
                    act.activation(cacc[:, c, :], cacc[:, c, :], ACT.Silu, bias=vcol("ln_b", c)).then_inc(s("conv_silu"), 1)
                for c in range(CC):
                    act.wait_ge(s("conv_silu"), c + 1)
                    act.activation(XH[:, 4 + c, :], cacc[:, c, :], ACT.Copy).then_inc(s("conv_hi"), 1)
                cast_to(("pw", 1))
                wait_full(act, ("pw", CC - 1))
                for c in range(CC):
                    src = wait_full(act, ("pw", c))
                    act.activation(XH[:, 4 + c, :], src[:, :], ACT.Copy).then_inc(s("pw_hi"), 1)

            def residual(j, m, unit_keys):
                for c in range(KD):
                    cast_to(unit_keys(c))
                    src = wait_full(act, ("y", j, c))
                    square(m, c, src[:, :])
                    act.activation(y[:, c, :], src[:, :], ACT.Copy).then_inc(frees(("y", j, c)), 1)
                root_mean(m)
                for c in range(KD):
                    act.wait_ge(s("resid"), j * KD + c + 1)
                    square(m + 1, c, hT[:, c, :])
                root_mean(m + 1)

            sil = y[:, 0:2, :]
            ff = y[:, 2:4, :]

            def feed_forward():
                high_of_norm(1)

                def high(c):
                    wait_read(act, ("fu", c))
                    act.activation(fH[:, c, :], ff[:, c % 2, :], ACT.Copy).then_inc(s("f_hi"), 1)

                for c in range(KF):
                    cast_to(("wg", c))
                    src = wait_full(act, ("fg", c))
                    if c >= 2:
                        wait_read(act, ("fu", c - 2))
                    act.activation(sil[:, c % 2, :], src[:, :], ACT.Silu).then_inc(frees(("fg", c)), 1)
                    cast_to(("wu", c))
                    if c >= 1:
                        high(c - 1)
                high(KF - 1)

            def store_out():
                for t in range(NT):
                    for half in range(2):
                        src = wait_full(act, ("out", t, half))
                        at = t * D + half * 512
                        act.activation(o_sb[:, at:at + 512], src[:, :], ACT.Copy).then_inc(frees(("out", t, half)), 1)

            def act_link(ins):
                act_links[0] += 1
                ins.then_inc(s("act_link"), 1)
                act.wait_ge(s("act_link"), act_links[0])

            act_links = [0]

            def root(dst, src, n, signal):
                act.activation(dst, src, ACT.Sqrt, bias=eps[:, 0:1], scale=1.0 / n).then_inc(s(signal), 1)

            def second_projections():
                high_of_norm(2)
                for f in range(2):
                    act.wait_ge(s("angles"), f + 1)
                    act.activation(cosin[:, f, :, :].rearrange("p t n -> p (t n)"), rt_angle(f), ACT.Sin).then_inc(
                        s("trig"), 1)
                for c in range(4):
                    cast_to(("u2", c))
                    src = wait_full(act, ("u2", c))
                    act.activation(ug[:, c, :], src[:, :], ACT.Gelu_apprx_tanh).then_inc(frees(("u2", c)), 1)
                cast_to(("ci", 3))
                for t in range(NT):
                    src = wait_full(act, ("ci", t))
                    act.activation(vga[:, t, 0:256], src[:, 0:256], ACT.Square, accum_out=css[:, t:t + 1])
                    act.activation(qi[:, t, 0:4, :], src[:, 256:512].rearrange("p (h d) -> p h d", h=4), ACT.Copy)
                    act.activation(ck[:, t, :], src[:, 0:256], ACT.Copy).then_inc(frees(("ci", t)), 1)
                wait_read(act, ("ci", NT - 1))
                root(crs, css, 256, "c_root")
                cast_to(("kw", 0))
                src = wait_full(act, ("kw", 0))
                kw = src[:, 0:NT * 68].rearrange("p (t n) -> p t n", t=NT)
                act.activation(qi[:, :, 4, :], kw[:, :, 0:64], ACT.Copy)
                act.activation(widx[:, :, :], kw[:, :, 64:68], ACT.Copy, scale=0.5).then_inc(frees(("kw", 0)), 1)
                cast_to(("qn", 3))
                for t in range(NT):
                    src = wait_full(act, ("qn", t))
                    act.activation(qk[:, t, 0:4, :], src[:, :].rearrange("p (h d) -> p h d", h=4), ACT.Copy).then_inc(
                        frees(("qn", t)), 1)
                for j in range(2):
                    src = wait_full(act, ("cT", j))
                    act.activation(cnT[:, j, :], src[:, :], ACT.Copy).then_inc(frees(("cT", j)), 1)
                cast_to(("vn", 3))
                act.wait_ge(s("rotated"), 1)
                for t in range(NT):
                    src = wait_full(act, ("vn", t))
                    act.activation(vga[:, t, :], src[:, :], ACT.Gelu_apprx_tanh, accum_out=vsum[:, t:t + 1]).then_inc(
                        frees(("vn", t)), 1)
                for i in range(2):
                    src = wait_full(act, ("kv", i))
                    kv = src[:, :].rearrange("p (t j n) -> p t j n", t=2, j=2)
                    act.activation(qk[:, 2 * i:2 * i + 2, 4, :], kv[:, :, 0, :], ACT.Copy)
                    act.activation(vv[:, 2 * i:2 * i + 2, :], kv[:, :, 1, :], ACT.Copy).then_inc(frees(("kv", i)), 1)
                act.wait_ge(s("v_mean"), 1)
                for t in range(NT):
                    act_link(act.activation(rl[:, t % 2, :], vga[:, t, :], ACT.Square, bias=nmean[:, t:t + 1],
                                            accum_out=vss[:, t:t + 1]))
                root(vrs, vss, T, "v_root")
                act.wait_ge(s("k_squares"), 1)
                root(krs, kss, P, "k_root")

            def second_transposes():
                src = wait_full(act, ("wT", 0))
                act.activation(wT[:, :, :], src[:, :].rearrange("p (g n) -> p g n", g=GR), ACT.Copy).then_inc(
                    frees(("wT", 0)), 1)
                for h in range(3):
                    src = wait_full(act, ("iT", h))
                    act.activation(qiT[:, h, :], src[:, :], ACT.Copy).then_inc(frees(("iT", h)), 1)
                for h in range(5):
                    src = wait_full(act, ("hT", h))
                    act.activation(qkT[:, h, :], src[:, :], ACT.Copy).then_inc(frees(("hT", h)), 1)

            def sparse_attention():
                for b in range(NT):
                    n = (b + 1) * P
                    for h in range(4):
                        src = wait_full(act, ("ix", b, h))
                        if 4 * b + h >= 2:
                            act.wait_ge(s("index_added"), 4 * b + h - 1)
                        act.activation(rl[:, h % 2, 0:n], src[:, 0:n], ACT.Relu, scale=HD ** -0.5).then_inc(
                            frees(("ix", b, h)), 1)
                    for c in range(4 * b, 4 * b + 4):
                        cast_to(("gt", c))
                        src = wait_full(act, ("gt", c))
                        act.activation(gt[:, c, :], src[:, :], ACT.Sigmoid).then_inc(frees(("gt", c)), 1)
                    act.wait_ge(s("amax"), b + 1)
                    for h in range(4):
                        last = act.activation(vga[:, h, 0:n], vga[:, h, 0:n], ACT.Exp, bias=amax[:, h:h + 1],
                                              accum_out=ansum[:, h:h + 1])
                    last.then_inc(s("exps2"), 1)
                    for kt in range(b + 1):
                        src = wait_full(act, ("pT2", b, kt))
                        if kt == 0 and b:
                            wait_full(act, ("yb", b - 1))
                        act.activation(pT2[:, kt, :, :].rearrange("p h q -> p (h q)"), src[:, :], ACT.Copy).then_inc(
                            frees(("pT2", b, kt)), 1)
                    src = wait_full(act, ("yb", b))
                    act.activation(qkT[:, 0:4, b * P:(b + 1) * P], src[:, :].rearrange("p (h q) -> p h q", h=4),
                                   ACT.Copy).then_inc(frees(("yb", b)), 1)

            def merge_and_out():
                wait_full(act, ("gt", 2 * KD - 1))
                act.wait_ge(s("gated_u"), NT)
                for c in range(4):
                    act.activation(XH[:, c, :], ug[:, c, :], ACT.Copy).then_inc(s("branch_hi"), 1)
                wait_read(act, ("yb", NT - 1))
                for c in range(4):
                    act.activation(XH[:, 4 + c, :], qkT[:, c, :], ACT.Copy).then_inc(s("branch_hi"), 1)
                cast_to(("wb", 3))
                wait_full(act, ("wb", KD - 1))
                for c in range(KD):
                    act.wait_ge(s("merged"), c + 1)
                    act.activation(XH[:, c, :], y[:, c, :], ACT.Copy).then_inc(s("merged_hi"), 1)
                for c in range(KD):
                    cast_to(("wo2", c))
                    if c < RING:
                        wait_read(act, ("o2", c))
                        square(6, c, hT[:, c, :])
                for c in range(RING, KD):
                    wait_read(act, ("o2", c))
                    square(6, c, hT[:, c, :])
                root_mean(6)

            def ranked_by(hp):
                return hp // 2 * 3 + hp % 2 + 1

            def choose_experts():
                high_of_norm(3)
                for q in range(4):
                    src = wait_full(act, ("sk", q))
                    act.activation(skT[:, 4 * q:4 * q + 4, :].rearrange("p a b -> p (a b)"), src[:, :], ACT.Copy).then_inc(
                        frees(("sk", q)), 1)

                def sub(hp):
                    src = wait_full(act, ("sub", hp))
                    if hp >= 4:
                        act.wait_ge(s("ranked"), ranked_by(hp - 4))
                    act.activation(subs[:, hp % 4, :, :].rearrange("p a b -> p (a b)"), src[:, :], ACT.Copy).then_inc(
                        frees(("sub", hp)), 1)

                for hp in range(2 * PH):
                    cast_to(("wq", hp))
                    src = wait_full(act, ("q2", hp))
                    if hp >= 2:
                        wait_full(act, ("sub", hp - 2))
                    act.activation(qq[:, hp % 2, :], src[:, :], ACT.Copy).then_inc(frees(("q2", hp)), 1)
                    if hp:
                        sub(hp - 1)
                sub(2 * PH - 1)
                act.wait_ge(s("best_less_max"), 1)
                flat = best[:, :, :, :].rearrange("p a b c -> p (a b c)")
                act.activation(flat, flat, ACT.Exp).then_inc(s("gate_exps"), 1)
                for t in range(NT):
                    src = wait_full(act, ("sel", t))
                    tok = slice(t * P, (t + 1) * P)
                    act.activation(ijcol[:, 0, tok], src[:, 0:P], ACT.Copy)
                    act.activation(ijcol[:, 1, tok], src[:, P:2 * P], ACT.Copy)
                    act.activation(gcol[:, tok], src[:, 2 * P:3 * P], ACT.Copy).then_inc(frees(("sel", t)), 1)

            def gate_matrices():
                act.sem_inc(s("g_copied"), NQ)
                for tt in range(NGT):
                    if tt >= 2:
                        act.wait_ge(s(f"g_out{tt - 2}"), 16)
                    with act.Fori(0, GTOK // (NQ * TOK4)) as n:
                        for q in range(NQ):
                            four = n * NQ + (tt * GTOK // TOK4 + q)
                            act.wait_ge(s("g_full"), four + NQ + 1)
                            to = Gs[:, tt % 2, :, bass.ds(n * (NQ * TOK4) + q * TOK4, TOK4)]
                            act.activation(to.rearrange("p i t -> p t i"),
                                           banks[q][:, :].rearrange("p (t i) -> p t i", t=TOK4), ACT.Copy).then_inc(
                                               s("g_copied"), 1)

            def experts():
                def high_u(x, b):
                    act.wait_ge(s("up_full"), x + 1)
                    for half in range(2):
                        act.wait_ge(s("ut_full"), x * 2 + half + 1)
                        act.activation(UH[:, b, half * 4:half * 4 + 4, :].rearrange("p a b -> p (a b)"),
                                       banks[half][:, :], ACT.Copy).then_inc(s("ut_hi"), 1)

                def high_v(x, e, g):
                    act.wait_ge(s(f"v_landed{e}"), g * 16 + 16)
                    act.wait_ge(s("down_full"), g * KD + 1)
                    act.activation(VH[:, e, :], vraw[:, e, :], ACT.Copy).then_inc(s("v_hi"), 1)

                def activate(x, b):
                    act.wait_ge(s("up_full"), x + 3)
                    act.wait_ge(s("ga_f"), x + 1)
                    act.activation(ac[:, b, :], banks[2 + b][:, :], ACT.Gelu_apprx_tanh).then_inc(s("gelu"), 1)

                def high_a(x, e, g):
                    act.wait_ge(s("ga_f"), x + 3)
                    act.wait_ge(s("down_full"), g * KD + 1)
                    act.activation(GH[:, e, :], ga[:, e % 2, :], ACT.Copy).then_inc(s("ga_hi"), 1)

                act.sem_inc(s("gelu"), 2)
                high_u(0, 0)
                high_u(1, 1)
                activate(0, 0)
                for tt in (NGT - 2, NGT - 1):
                    act.wait_ge(s(f"g_out{tt}"), 16)
                high_v(0, 0, 0)
                high_a(0, 0, 0)
                with act.Fori(0, LAST) as g:
                    for e in range(1, EG + 1):
                        x = g * EG + e
                        group = g if e < EG else g + 1
                        high_u(x + 1, (e + 1) % 2)
                        if e < EG:
                            high_v(x, e, group)
                            activate(x, e % 2)
                            high_a(x, e, group)
                        else:
                            activate(x, 0)
                            high_a(x, 0, group)
                            high_v(x, 0, group)
                for x in range(LAST * EG + 1, NEXP):
                    if x + 1 < NEXP:
                        high_u(x + 1, (x + 1) % 2)
                    high_v(x, x % EG, LAST)
                    activate(x, x % 2)
                    high_a(x, x % EG, LAST)

            prepare()
            first_projections()
            attention()
            conv_tail()
            residual(0, 2, lambda c: ("wo", c))
            feed_forward()
            residual(1, 4, lambda c: ("wd", c, 2))
            second_projections()
            second_transposes()
            sparse_attention()
            merge_and_out()
            choose_experts()
            gate_matrices()
            experts()
            store_out()

        @block.vector
        def _(dve):
            links = [0]

            def link(ins):
                links[0] += 1
                ins.then_inc(s("dve_link"), 1)
                dve.wait_ge(s("dve_link"), links[0])

            def step(ins):
                ins.then_inc(s("dve_link"), 1)
                links[0] += 1
                return links[0]

            def inverse_root(m):
                wait_read(dve, ("ss", m))
                link(dve.reciprocal(rstd[:, :], rt[:, :]))

            def norm(n, m, gain):
                def low(k):
                    dve.wait_ge(s("x_hi"), n * KD + k + 1)
                    dve.tensor_tensor(XL[:, k, :], xn[:, k % RING, :], XH[:, k, :].bitcast(F32), ALU.subtract).then_inc(
                        s("x_lo"), 1)

                inverse_root(m)
                for k in range(KD):
                    if n * KD + k >= RING:
                        dve.wait_ge(s("x_lo"), n * KD + k - RING + 1)
                    dve.scalar_tensor_tensor(out=xn[:, k % RING, :], in0=hT[:, k, :], scalar=vcol(gain, k),
                                             in1=rstd[:, :], op0=ALU.mult, op1=ALU.mult).then_inc(s("xn"), 1)
                    if k >= 1:
                        low(k - 1)
                low(KD - 1)

            def prepare():
                dve.memset(hpad[:, :, 0:TAPS - 1], 0.0)
                dve.memset(relb[BUCKETS:BUCKETS + 1, :], NEG).then_inc(s("dve_link"), 1)
                links[0] += 1
                dve.wait_ge(s("dve_link"), links[0])
                dve.wait_ge(s("relb_landed"), 32)
                dve.tensor_copy(relbB[:, :, :], relb[:, :].unsqueeze(2).to_broadcast([BUCKETS + 1, NH, P])).then_inc(
                    s("relb_spread"), 1)
                src = wait_full(dve, ("vec", 0))
                dve.tensor_copy(vec[:, 0:NV], src[:, 0:NV]).then_inc(frees(("vec", 0)), 1)
                src = wait_full(dve, ("vec", 1))
                dve.tensor_copy(taps[:, 0:TAPS * CC], src[:, 0:TAPS * CC]).then_inc(frees(("vec", 1)), 1)
                wait_read(dve, ("vec", 0))
                wait_read(dve, ("vec", 1))
                norm(0, 0, "mix_pre")

            def convolution():
                def gated(c):
                    wait_read(dve, ("cg", c))
                    src = wait_full(dve, ("ca", c))
                    dve.tensor_tensor(hpad[:, c, TAPS - 1:], src[:, :], sg[:, c % 2, :], ALU.mult).then_inc(
                        frees(("ca", c)), 1)

                before = {}

                def tap(c, w):
                    if w == 0:
                        gated(c)
                        wait_read(dve, ("ca", c))
                        before[c] = step(dve.tensor_scalar(cacc[:, c, :], hpad[:, c, 0:T], taps[:, c:c + 1],
                                                           vcol("dw_b", c), ALU.mult, ALU.add))
                        return
                    dve.wait_ge(s("dve_link"), before[c])
                    done = dve.scalar_tensor_tensor(out=cacc[:, c, :], in0=hpad[:, c, w:w + T],
                                                    scalar=taps[:, w * CC + c:w * CC + c + 1],
                                                    in1=cacc[:, c, :], op0=ALU.mult, op1=ALU.add)
                    if w < TAPS - 1:
                        before[c] = step(done)
                    else:
                        done.then_inc(s("conv_done"), 1)

                alone = TAPS // 2
                for w in range(alone):
                    tap(0, w)
                for c in range(CC - 2):
                    for w in range(alone, TAPS):
                        tap(c, w)
                        if w - alone < alone:
                            tap(c + 1, w - alone)
                        if c == CC - 3 and w == alone:
                            gated(CC - 1)
                for w in range(alone, TAPS):
                    tap(CC - 2, w)

            def attention():
                dve.wait_ge(s("bias_landed"), 16)
                dve.wait_ge(s("sinks_landed"), 16)

                def logits(b):
                    w = P if b == 0 else 2 * P
                    per = 512 // w
                    st = st1[:, b % 2]
                    for i in range(NH // per):
                        src = wait_full(dve, ("sc", b, i))
                        if b >= 2 and i == 0:
                            wait_full(dve, ("pT", b - 2, 3))
                        heads = heads_of(i, per)
                        dve.scalar_tensor_tensor(out=sc1[:, b % 2, heads, 0:w],
                                                 in0=src[:, :].rearrange("p (j w) -> p j w", w=w), scalar=HD ** -0.5,
                                                 in1=biasT[:, heads, 2 * P - w:2 * P],
                                                 op0=ALU.mult, op1=ALU.add).then_inc(frees(("sc", b, i)), 1)
                    wait_read(dve, ("sc", b, NH // per - 1))
                    link(dve.tensor_reduce(st[:, 0, :], sc1[:, b % 2, :, 0:w], AX_X, ALU.max))
                    link(dve.tensor_tensor(st[:, 0, :], st[:, 0, :], sinkb[:, :], ALU.max))
                    dve.tensor_scalar(st[:, 1, :], st[:, 0, :], -1.0, None, ALU.mult)
                    dve.tensor_tensor(st[:, 3, :], sinkb[:, :], st[:, 0, :], ALU.subtract).then_inc(s("sink_gap"), 1)

                def normalise(b):
                    w = P if b == 0 else 2 * P
                    st = st1[:, b % 2]
                    dve.wait_ge(s("exps"), b + 1)
                    link(dve.tensor_tensor(st[:, 5, :], st[:, 2, :], st[:, 4, :], ALU.add))
                    link(dve.reciprocal(st[:, 6, :], st[:, 5, :]))
                    pr = sc1[:, b % 2, :, 0:w]
                    dve.tensor_tensor(pr, pr, st[:, 6, :].unsqueeze(2).to_broadcast([P, NH, w]), ALU.mult).then_inc(
                        s("probs"), 1)

                def low(b):
                    dve.wait_ge(s("att_hi"), b + 1)
                    src = wait_full(dve, ("o", b))
                    to = slice(b * P, (b + 1) * P)
                    dve.tensor_tensor(XL[:, 0:4, to], src[:, :].rearrange("p (c q) -> p c q", c=4),
                                      XH[:, 0:4, to].bitcast(F32), ALU.subtract).then_inc(frees(("o", b)), 1)

                logits(0)
                for b in range(NT):
                    if b + 1 < NT:
                        logits(b + 1)
                    normalise(b)
                    if b:
                        low(b - 1)
                low(NT - 1)

            def conv_tail():
                src = wait_full(dve, ("cmean", 0))
                dve.tensor_scalar(cln[:, 0, :], src[:, :], 1.0 / (CC * P), None, ALU.mult).then_inc(frees(("cmean", 0)), 1)
                wait_read(dve, ("cmean", 0))
                for c in range(CC):
                    dve.tensor_tensor(cacc[:, c, :], cacc[:, c, :], cln[:, 0, :], ALU.subtract).then_inc(s("centred"), 1)
                inverse_root(1)
                for c in range(CC):
                    dve.scalar_tensor_tensor(out=cacc[:, c, :], in0=cacc[:, c, :], scalar=vcol("ln_g", c),
                                             in1=rstd[:, :], op0=ALU.mult, op1=ALU.mult).then_inc(s("ln_scaled"), 1)
                for c in range(CC):
                    dve.wait_ge(s("conv_hi"), c + 1)
                    dve.tensor_tensor(XL[:, 4 + c, :], cacc[:, c, :], XH[:, 4 + c, :].bitcast(F32), ALU.subtract).then_inc(
                        s("conv_lo"), 1)
                for c in range(CC):
                    dve.wait_ge(s("pw_hi"), c + 1)
                    src = wait_full(dve, ("pw", c))
                    dve.tensor_tensor(XL[:, 4 + c, :], src[:, :], XH[:, 4 + c, :].bitcast(F32), ALU.subtract).then_inc(
                        frees(("pw", c)), 1)

            def residual(j, m, gain):
                def add(c):
                    dve.wait_ge(s("y_scaled"), j * KD + c + 1)
                    dve.tensor_tensor(hT[:, c, :], hT[:, c, :], y[:, c, :], ALU.add).then_inc(s("resid"), 1)

                inverse_root(m)
                for c in range(KD):
                    dve.scalar_tensor_tensor(out=y[:, c, :], in0=y[:, c, :], scalar=vcol(gain, c), in1=rstd[:, :],
                                             op0=ALU.mult, op1=ALU.mult).then_inc(s("y_scaled"), 1)
                    if c:
                        add(c - 1)
                add(KD - 1)

            sil = y[:, 0:2, :]
            ff = y[:, 2:4, :]

            def feed_forward():
                def low(c):
                    dve.wait_ge(s("f_hi"), c + 1)
                    dve.tensor_tensor(fL[:, c, :], ff[:, c % 2, :], fH[:, c, :].bitcast(F32), ALU.subtract).then_inc(
                        s("f_lo"), 1)

                for c in range(KF):
                    wait_read(dve, ("fg", c))
                    src = wait_full(dve, ("fu", c))
                    if c >= 2:
                        dve.wait_ge(s("f_lo"), c - 1)
                    dve.tensor_tensor(ff[:, c % 2, :], src[:, :], sil[:, c % 2, :], ALU.mult).then_inc(frees(("fu", c)), 1)
                    if c:
                        low(c - 1)
                low(KF - 1)

            def angles():
                dve.wait_ge(s("pos_landed"), 32)
                link(dve.tensor_copy(posf[:, :], posi[:, :]))
                ang = rl[:, 0, 0:NT * NROT]
                turns = rl[:, 0, 128:128 + NT * NROT]
                link(dve.tensor_tensor(ang.rearrange("p (t n) -> p t n", t=NT),
                                       posf[:, :].unsqueeze(2).to_broadcast([P, NT, NROT]),
                                       invb[:, :].unsqueeze(1).to_broadcast([P, NT, NROT]), ALU.mult))
                for f in range(2):
                    quarter = 0.25 if f == 0 else 0.0
                    r = rt_angle(f)
                    link(dve.tensor_scalar(turns, ang, 1.0 / (2 * math.pi), quarter, ALU.mult, ALU.add))
                    link(dve.tensor_scalar(turns, turns, ROUND, -ROUND, ALU.add, ALU.add))
                    link(dve.scalar_tensor_tensor(out=r, in0=turns, scalar=-TURN[0], in1=ang, op0=ALU.mult, op1=ALU.add))
                    for part in TURN[1:]:
                        link(dve.scalar_tensor_tensor(out=r, in0=turns, scalar=-part, in1=r, op0=ALU.mult, op1=ALU.add))
                    link(dve.tensor_scalar(r, r, quarter * 2 * math.pi, PI_BELOW, ALU.add, ALU.min))
                    dve.tensor_scalar(r, r, -PI_BELOW, None, ALU.max).then_inc(s("angles"), 1)

            def rotate(x, half, at, heads, signal=None):
                x1, x2 = x[:, :, 0:heads, 0:half], x[:, :, 0:heads, half:2 * half]
                c, sn = (cosin[:, f, :, at:at + half].unsqueeze(2).to_broadcast([P, NT, heads, half]) for f in range(2))
                n = NT * heads * half
                tmp = [vga[:, j, 0:n].rearrange("p (t h d) -> p t h d", t=NT, h=heads) for j in range(4)]
                dve.tensor_tensor(tmp[0], x1, c, ALU.mult)
                dve.tensor_tensor(tmp[1], x2, sn, ALU.mult)
                dve.tensor_tensor(tmp[2], x2, c, ALU.mult)
                link(dve.tensor_tensor(tmp[3], x1, sn, ALU.mult))
                dve.tensor_tensor(x1, tmp[0], tmp[1], ALU.subtract)
                last = dve.tensor_tensor(x2, tmp[2], tmp[3], ALU.add)
                last.then_inc(signal, 1) if signal else link(last)

            def second_projections():
                angles()
                dve.wait_ge(s("gains_landed"), 6 * 16)
                dve.wait_ge(s("c_root"), 1)
                link(dve.reciprocal(crs, crs))
                for t in range(NT):
                    dve.scalar_tensor_tensor(out=ck[:, t, :], in0=ck[:, t, :], scalar=crs[:, t:t + 1], in1=gkv[:, :],
                                             op0=ALU.mult, op1=ALU.mult).then_inc(s("cn_made"), 1)
                wait_read(dve, ("kw", 0))
                dve.wait_ge(s("trig"), 2)
                rotate(qi, 8, 16, 5)
                dve.tensor_copy(qi[:, :, 5, :], qi[:, :, 4, :]).then_inc(s("rotated"), 1)

            def second_norms():
                for t in range(NT):
                    wait_read(dve, ("vn", t))
                link(dve.tensor_scalar(vmean, vsum, 1.0 / T, None, ALU.mult))
                dve.tensor_scalar(nmean, vmean, -1.0, None, ALU.mult).then_inc(s("v_mean"), 1)
                dve.wait_ge(s("v_root"), 1)
                link(dve.reciprocal(vrs, vrs))
                for t in range(NT):
                    v = vga[:, t, :]
                    link(dve.tensor_scalar(v, v, vmean[:, t:t + 1], vrs[:, t:t + 1], ALU.subtract, ALU.mult))
                    link(dve.tensor_tensor(v, v, gvb[:, 0, :], ALU.mult))
                    dve.tensor_tensor(v, v, gvb[:, 1, :], ALU.add).then_inc(s("v_normed"), 1)
                for t in range(NT):
                    wait_read(dve, ("qn", t))
                for i in range(2):
                    wait_read(dve, ("kv", i))
                for t in range(NT):
                    sqs = gt[:, 8 + 2 * t:8 + 2 * t + 2, :].rearrange("p a b -> p (a b)")[:, 0:5 * P].rearrange(
                        "p (h d) -> p h d", h=5)
                    link(dve.tensor_tensor(sqs, qk[:, t, :, :], qk[:, t, :, :], ALU.mult))
                    last = dve.tensor_reduce(kss[:, 5 * t:5 * t + 5], sqs, AX_X, ALU.add)
                last.then_inc(s("k_squares"), 1)
                dve.wait_ge(s("k_root"), 1)
                link(dve.reciprocal(krs, krs))
                for t in range(NT):
                    x = qk[:, t, :, :]
                    link(dve.tensor_tensor(x, x, krs[:, 5 * t:5 * t + 5].unsqueeze(2).to_broadcast([P, 5, P]), ALU.mult))
                    dve.tensor_tensor(x[:, 0:4, :], x[:, 0:4, :], gqk[:, 0:1, :].to_broadcast([P, 4, P]), ALU.mult)
                    link(dve.tensor_tensor(x[:, 4, :], x[:, 4, :], gqk[:, 1, :], ALU.mult))
                for t in range(NT):
                    src = wait_full(dve, ("z", t))
                    tok = slice(t * P, (t + 1) * P)
                    z = gt[:, 8 + t, :].rearrange("p (g n) -> p g n", g=GR)
                    dve.tensor_tensor(z, src[:, :].rearrange("p (g n) -> p g n", g=GR), bsb[:, :, :], ALU.add).then_inc(
                        frees(("z", t)), 1)
                    wait_read(dve, ("z", t))
                    dve.tensor_tensor(ug[:, :, tok], ug[:, :, tok], z, ALU.mult).then_inc(s("gated_u"), 1)
                dve.wait_ge(s("gated_u"), NT)
                rotate(qk, 16, 0, 5, s("rotated"))

            def sparse_attention():
                for b in range(NT):
                    n = (b + 1) * P
                    sc = isc[:, 0:n]
                    for h in range(4):
                        wait_read(dve, ("ix", b, h))
                        w = widx[:, b, h:h + 1]
                        if h == 0:
                            add = dve.tensor_scalar(sc, rl[:, 0, 0:n], w, None, ALU.mult)
                        else:
                            dve.wait_ge(s("index_added"), 4 * b + h)
                            add = dve.scalar_tensor_tensor(out=sc, in0=rl[:, h % 2, 0:n], scalar=w, in1=sc,
                                                           op0=ALU.mult, op1=ALU.add)
                        add.then_inc(s("index_added"), 1)
                    dve.wait_ge(s("index_added"), 4 * b + 4)
                    if b == 0:
                        dve.wait_ge(s("causal_made"), 2)
                        link(dve.tensor_copy(madd[:, 0:n], causal[:, :]))
                    else:
                        link(dve.tensor_tensor(sc[:, b * P:n], sc[:, b * P:n], causal[:, :], ALU.add))
                        for _ in range(TOPK // 8):
                            link(dve.max(m8[:, :], sc))
                            link(dve.match_replace(out=sc, in_to_replace=m8[:, :], in_values=sc, imm_value=TAKEN))
                        link(dve.tensor_scalar(madd[:, 0:n], sc, TAKEN / 2, NEG, ALU.is_gt, ALU.mult))
                    for h in range(4):
                        src = wait_full(dve, ("at", b, h))
                        dve.scalar_tensor_tensor(out=vga[:, h, 0:n], in0=src[:, 0:n], scalar=P ** -0.5,
                                                 in1=madd[:, 0:n], op0=ALU.mult, op1=ALU.add).then_inc(
                                                     frees(("at", b, h)), 1)
                    for h in range(4):
                        wait_read(dve, ("at", b, h))
                    link(dve.tensor_reduce(amax, vga[:, :, 0:n], AX_X, ALU.max))
                    dve.tensor_scalar(amax, amax, -1.0, None, ALU.mult).then_inc(s("amax"), 1)
                    dve.wait_ge(s("exps2"), b + 1)
                    link(dve.reciprocal(arec, ansum))
                    dve.tensor_tensor(vga[:, :, 0:n], vga[:, :, 0:n], arec.unsqueeze(2).to_broadcast([P, 4, n]),
                                      ALU.mult).then_inc(s("probs2"), 1)

            def merge_and_out():
                for c in range(KD):
                    src = ug[:, c, :] if c < 4 else qkT[:, c - 4, :]
                    dve.wait_ge(s("branch_hi"), c + 1)
                    dve.tensor_tensor(XL[:, c, :], src, XH[:, c, :].bitcast(F32), ALU.subtract).then_inc(
                        s("branch_lo"), 1)
                for c in range(KD):
                    wait_read(dve, ("gt", c))
                    wait_read(dve, ("gt", KD + c))
                    src = wait_full(dve, ("wa", c))
                    dve.tensor_tensor(y[:, c, :], src[:, :], gt[:, c, :], ALU.mult).then_inc(frees(("wa", c)), 1)
                    src = wait_full(dve, ("wb", c))
                    dve.tensor_tensor(gt[:, KD + c, :], src[:, :], gt[:, KD + c, :], ALU.mult).then_inc(
                        frees(("wb", c)), 1)
                    wait_read(dve, ("wa", c))
                    wait_read(dve, ("wb", c))
                    dve.tensor_tensor(y[:, c, :], y[:, c, :], gt[:, KD + c, :], ALU.add).then_inc(s("merged"), 1)
                for c in range(KD):
                    dve.wait_ge(s("merged_hi"), c + 1)
                    dve.tensor_tensor(XL[:, c, :], y[:, c, :], XH[:, c, :].bitcast(F32), ALU.subtract).then_inc(
                        s("merged_lo"), 1)
                for c in range(KD):
                    src = wait_full(dve, ("o2", c))
                    dve.tensor_tensor(hT[:, c, :], hT[:, c, :], src[:, :], ALU.add).then_inc(frees(("o2", c)), 1)

            def best16(src, work, values, indices, made, ranked):
                first, rest, second = {}, {}, {}
                for t in range(NT):
                    if made:
                        dve.wait_ge(s("dve_link"), made[t])
                    first[t] = step(dve.max(values(t, 0), src(t)))
                if ranked:
                    dve.wait_ge(s("ranked"), ranked)
                for t in range(NT):
                    dve.wait_ge(s("dve_link"), first[t])
                    dve.max_index(indices(t, 0), values(t, 0), src(t))
                    rest[t] = step(dve.match_replace(out=work(t), in_to_replace=values(t, 0), in_values=src(t),
                                                     imm_value=TAKEN))
                for t in range(NT):
                    dve.wait_ge(s("dve_link"), rest[t])
                    second[t] = step(dve.max(values(t, 1), work(t)))
                for t in range(NT):
                    dve.wait_ge(s("dve_link"), second[t])
                    last = dve.max_index(indices(t, 1), values(t, 1), work(t))
                last.then_inc(s("ranked"), 1)

            def choose_experts():
                ranked = [0]

                def best_of_part(hp):
                    wait_read(dve, ("sub", hp))
                    best16(lambda t: subs[:, hp % 4, t, :], lambda t: wk[:, t, 0:P],
                           lambda t, i: stop[:, t, hp, 8 * i:8 * i + 8], lambda t, i: itop[:, t, hp, 8 * i:8 * i + 8],
                           None, ranked[0])
                    ranked[0] += 1

                def best_of_sums(h):
                    n, a, b = WIDE * SEL, stop[:, :, 2 * h, :], stop[:, :, 2 * h + 1, 0:NARROW]
                    dve.tensor_tensor(cand[:, :, 0:n].rearrange("p t (a b) -> p t a b", a=WIDE),
                                      a[:, :, 0:WIDE].unsqueeze(3).to_broadcast([P, NT, WIDE, SEL]),
                                      stop[:, :, 2 * h + 1, :].unsqueeze(2).to_broadcast([P, NT, WIDE, SEL]), ALU.add)
                    made = [step(dve.tensor_tensor(
                        cand[:, :, n:NSUM].rearrange("p t (a b) -> p t a b", a=SEL - WIDE),
                        a[:, :, WIDE:SEL].unsqueeze(3).to_broadcast([P, NT, SEL - WIDE, NARROW]),
                        b.unsqueeze(2).to_broadcast([P, NT, SEL - WIDE, NARROW]), ALU.add))] * NT
                    best16(lambda t: cand[:, t, :], lambda t: wk[:, t, 0:NSUM],
                           lambda t, i: best[:, t, h, 8 * i:8 * i + 8],
                           lambda t, i: bpos[:, t, h, 8 * i:8 * i + 8], made, ranked[0])
                    ranked[0] += 1

                split_at = {}

                def split_rank(h):
                    dve.wait_ge(s("ranked"), 3 * h + 3)
                    for j, (by, op) in enumerate(((4, ALU.logical_shift_right), (SEL - 1, ALU.bitwise_and),
                                                  (2, ALU.logical_shift_right), (NARROW - 1, ALU.bitwise_and),
                                                  (6, ALU.logical_shift_right))):
                        dve.tensor_scalar(bits[:, h % 2, j, :].rearrange("p (t s) -> p t s", t=NT), bpos[:, :, h, :],
                                          by, None, op)
                    split_at[h] = step(dve.tensor_copy(itf[:, h, :, :].rearrange("p (a t) s -> p a t s", a=2),
                                                       itop[:, :, 2 * h:2 * h + 2, :].rearrange("p t a s -> p a t s")))

                def rank_number(h):
                    dve.wait_ge(s("dve_link"), split_at[h])
                    split_at[h] = step(dve.tensor_copy(bitf[:, h % 2, :, :].rearrange("p a n -> p (a n)"),
                                                       bits[:, h % 2, :, :].rearrange("p a n -> p (a n)")))

                def rank_difference(h):
                    dve.wait_ge(s("dve_link"), split_at[h])
                    at = bitf[:, h % 2]
                    dve.scalar_tensor_tensor(out=bdif[:, h % 2, 0, :], in0=at[:, 2, :],
                                             scalar=float(WIDE - WIDE * SEL // NARROW), in1=at[:, 0, :],
                                             op0=ALU.add, op1=ALU.subtract)
                    split_at[h] = step(dve.tensor_tensor(bdif[:, h % 2, 1, :], at[:, 3, :], at[:, 1, :], ALU.subtract))

                def ranks(h):
                    dve.wait_ge(s("dve_link"), split_at[h])
                    at, dif = bitf[:, h % 2], bdif[:, h % 2, :, :]
                    link(dve.tensor_tensor(dif, dif, at[:, 4, :].unsqueeze(1).to_broadcast([P, 2, NT * SEL]), ALU.mult))
                    dve.tensor_tensor(bhf[:, h, :, :, :].rearrange("p a t s -> p a (t s)"), at[:, 0:2, :], dif,
                                      ALU.add).then_inc(s("ranks"), 1)

                def rank_hot(h):
                    dve.wait_ge(s("ranks"), h + 1)
                    if h == 0:
                        dve.wait_ge(s("iota_made"), 1)
                    if h >= 2:
                        dve.wait_ge(s("summed"), h - 1)
                    dve.tensor_tensor(hot[:, h % 2, :, :, :].rearrange("p a s r -> p (a s) r"),
                                      bhf[:, h, :, :, :].rearrange("p a t s -> p (a t s)").unsqueeze(2).to_broadcast(
                                          [P, 2 * NT * SEL, SEL]),
                                      iota16[:, :].unsqueeze(1).to_broadcast([P, 2 * NT * SEL, SEL]),
                                      ALU.is_equal).then_inc(s("rank_hots"), 1)

                def sum_picked(h):
                    dve.wait_ge(s("picked"), h + 1)
                    dve.tensor_reduce(sel[:, 0:2, :, h * SEL:(h + 1) * SEL].rearrange("p a t s -> p (a t) s"),
                                      hot[:, h % 2, :, :, :], AX_X, ALU.add).then_inc(s("summed"), 1)

                norm(3, 6, "norm2")
                for h in range(PH):
                    best_of_part(2 * h)
                    if h:
                        split_rank(h - 1)
                    best_of_part(2 * h + 1)
                    if h:
                        rank_number(h - 1)
                    best_of_sums(h)
                    if h:
                        rank_difference(h - 1)
                    if h >= 2:
                        sum_picked(h - 2)
                    if h:
                        ranks(h - 1)
                        rank_hot(h - 1)
                split_rank(PH - 1)
                b3 = best[:, :, :, :].rearrange("p t h s -> p (t h) s")
                first_copied = step(dve.tensor_copy(bsum[:, :], b3[:, :, 0]))
                rank_number(PH - 1)
                dve.wait_ge(s("dve_link"), first_copied)
                dve.tensor_tensor(b3, b3, bsum[:, :].unsqueeze(2).to_broadcast([P, NT * PH, SEL]),
                                  ALU.subtract).then_inc(s("best_less_max"), 1)
                rank_difference(PH - 1)
                sum_picked(PH - 2)
                ranks(PH - 1)
                rank_hot(PH - 1)
                dve.wait_ge(s("gate_exps"), 1)
                link(dve.tensor_reduce(bsum[:, :], b3, AX_X, ALU.add))
                link(dve.reciprocal(bsum[:, :], bsum[:, :]))
                link(dve.tensor_tensor(sel[:, 2, :, :].rearrange("p t (h s) -> p (t h) s", h=PH), b3,
                                       bsum[:, :].unsqueeze(2).to_broadcast([P, NT * PH, SEL]), ALU.mult))
                sum_picked(PH - 1)

            def gate_matrices():
                dve.wait_ge(s("iota_made"), 2)
                for t in range(NT):
                    wait_read(dve, ("sel", t))
                for tt in range(NGT):
                    with dve.Fori(0, GTOK // (NQ * TOK4)) as n:
                        for q in range(NQ):
                            four = n * NQ + (tt * GTOK // TOK4 + q)
                            dve.wait_ge(s("g_full"), four + 1)
                            ij = ijcol[:, :, bass.ds(n * (NQ * TOK4) + (tt * GTOK + q * TOK4), TOK4)]
                            dve.tensor_tensor(hots[:, q, :, :, :],
                                              iota128[:, :].unsqueeze(1).unsqueeze(1).to_broadcast([P, 2, TOK4, P]),
                                              ij.unsqueeze(3).to_broadcast([P, 2, TOK4, P]), ALU.is_equal).then_inc(
                                                  s("hots_made"), 1)

            def experts():
                def low_u(x, b):
                    for half in range(2):
                        dve.wait_ge(s("ut_hi"), x * 2 + half + 1)
                        to = [w[:, b, half * 4:half * 4 + 4, :].rearrange("p a b -> p (a b)") for w in (UL, UH)]
                        dve.tensor_tensor(to[0], banks[half][:, :], to[1].bitcast(F32), ALU.subtract).then_inc(
                            s("ut_lo"), 1)

                def weigh(x, e, g):
                    dve.wait_ge(s("gelu"), x + 3)
                    dve.wait_ge(s(f"g_landed{e}"), g * 16 + 16)
                    dve.wait_ge(s("ga_lo"), x + 1)
                    dve.tensor_tensor(ga[:, e % 2, :], ac[:, e % 2, :], gr[:, e, :], ALU.mult).then_inc(s("ga_f"), 1)

                def low_a(x, e):
                    dve.wait_ge(s("ga_hi"), x + 1)
                    dve.tensor_tensor(GL[:, e, :], ga[:, e % 2, :], GH[:, e, :].bitcast(F32), ALU.subtract).then_inc(
                        s("ga_lo"), 1)

                def add(g):
                    for c in range(KD):
                        dve.wait_ge(s("down_full"), g * KD + c + 2)
                        dve.tensor_tensor(hT[:, c, :], hT[:, c, :], banks[4 + c % 2][:, :], ALU.add).then_inc(
                            s("added"), 1)

                for name in ("ut_lo", "ga_f", "ga_lo", "added"):
                    dve.sem_inc(s(name), 2)
                low_u(0, 0)
                low_u(1, 1)
                weigh(0, 0, 0)
                low_a(0, 0)
                with dve.Fori(0, LAST) as g:
                    for e in range(1, EG + 1):
                        x = g * EG + e
                        low_u(x + 1, (e + 1) % 2)
                        weigh(x, e % EG, g if e < EG else g + 1)
                        if e == EG:
                            add(g)
                        low_a(x, e % EG)
                for x in range(LAST * EG + 1, NEXP):
                    if x + 1 < NEXP:
                        low_u(x + 1, (x + 1) % 2)
                    weigh(x, x % EG, LAST)
                    low_a(x, x % EG)
                add(LAST)

            prepare()
            convolution()
            attention()
            conv_tail()
            residual(0, 2, "mix_post")
            norm(1, 3, "ffn_pre")
            feed_forward()
            residual(1, 4, "ffn_post")
            norm(2, 5, "norm1")
            second_projections()
            second_norms()
            sparse_attention()
            merge_and_out()
            choose_experts()
            gate_matrices()
            experts()


def kernel(**inputs):
    import numpy as _np
    import concourse.bacc as _bacc
    from concourse import mybir as _mybir
    from concourse.bass_utils import run_bass_kernel_spmd as _run

    nc = _bacc.Bacc("TRN2", target_bir_lowering=False, num_devices=1)
    onehot, inv = shape_constants()
    arrays, views = {}, {}
    for name, value in list(inputs.items()) + [("onehot_rows", onehot), ("inv_freq", inv)]:
        a = _np.ascontiguousarray(value)
        arrays[f"in_{name}"] = a
        views[name] = nc.dram_tensor(f"in_{name}", a.shape, _mybir.dt.from_np(a.dtype), kind="ExternalInput").ap()
    out = nc.dram_tensor("out", (1, T, D), F32, kind="ExternalOutput").ap()
    onehot_rows, inv_freq = views.pop("onehot_rows"), views.pop("inv_freq")
    block_pair_kernel(nc, views, onehot_rows, inv_freq, out)
    return _run(nc, [arrays], core_ids=[0]).results[0]["out"]
```
